# Optimizing a Trainium2 kernel written in Bass

```python
import jax, jax.numpy as jnp
from jax import lax
import numpy as np

D_MODEL = 1024
BATCH = 1
SEQ = 256
DEPTH = 2

CONV_WIDTH = 512
CONV_HEADS = 8
CONV_HEAD_DIM = CONV_WIDTH // CONV_HEADS
CONV_K = 3
GMLP_WIDTH = 512
GMLP_HEADS = 4
GMLP_HEAD_DIM = GMLP_WIDTH // GMLP_HEADS
CHUNK = 128
MIX_WIDTH = CONV_WIDTH + GMLP_WIDTH
IN_PROJ_WIDTH = 3 * CONV_WIDTH + 2 * GMLP_WIDTH
D_FF_DENSE = 2816
N_EXPERTS = 8
TOP_K = 2
D_FF_EXPERT = 3584
N_DENSE = (DEPTH + 1) // 2
N_MOE = DEPTH // 2
ALPHA = (2 * DEPTH) ** 0.25
BETA = (8 * DEPTH) ** -0.25
LN_EPS = 1e-5
RMS_EPS = 1e-6

kernel_name = "hybrid_conv_sgu_moe_deepnorm"

def layer_norm(x, g, b):
    xf = x.astype(jnp.float32)
    mu = jnp.mean(xf, axis=-1, keepdims=True)
    var = jnp.mean(jnp.square(xf - mu), axis=-1, keepdims=True)
    return ((xf - mu) * lax.rsqrt(var + LN_EPS)).astype(x.dtype) * g + b

def head_rms_norm(y, n_heads, head_dim):
    bsz, s, _ = y.shape
    yf = y.astype(jnp.float32).reshape(bsz, s, n_heads, head_dim)
    yf = yf * lax.rsqrt(jnp.mean(jnp.square(yf), axis=-1, keepdims=True) + RMS_EPS)
    return yf.reshape(bsz, s, n_heads * head_dim).astype(y.dtype)

def causal_short_conv(h, w):
    hp = jnp.pad(h, ((0, 0), (CONV_K - 1, 0), (0, 0)))
    return w[0] * hp[:, :-2] + w[1] * hp[:, 1:-1] + w[2] * hp[:, 2:]

def chunked_spatial_gating(u, v, v_g, v_b, w_s, b_s):
    bsz, s, _ = v.shape
    v = layer_norm(v, v_g, v_b)
    v = v.reshape(bsz, s // CHUNK, CHUNK, GMLP_HEADS, GMLP_HEAD_DIM)
    causal = jnp.tril(jnp.ones((CHUNK, CHUNK), dtype=bool))
    w_causal = jnp.where(causal, w_s, jnp.zeros_like(w_s))
    z = jnp.einsum("hts,bnshd->bnthd", w_causal, v) + b_s.T[None, None, :, :, None]
    return u * z.reshape(bsz, s, GMLP_WIDTH)

def hybrid_mixer(x, w_in, conv_w, v_g, v_b, w_s, b_s, out_g, w_out):
    proj = x @ w_in
    b_gate, c_gate, h, u, v = jnp.split(
        proj, [CONV_WIDTH, 2 * CONV_WIDTH, 3 * CONV_WIDTH, 3 * CONV_WIDTH + GMLP_WIDTH], axis=-1)
    y_conv = b_gate * causal_short_conv(c_gate * h, conv_w)
    y_sg = chunked_spatial_gating(jax.nn.gelu(u, approximate=False), jax.nn.gelu(v, approximate=False),
                                  v_g, v_b, w_s, b_s)
    y = jnp.concatenate([head_rms_norm(y_conv, CONV_HEADS, CONV_HEAD_DIM),
                         head_rms_norm(y_sg, GMLP_HEADS, GMLP_HEAD_DIM)], axis=-1) * out_g
    return y @ w_out

def swiglu(x, wg, wu, wd):
    return (jax.nn.silu(x @ wg) * (x @ wu)) @ wd

def moe_swiglu(x, w_router, we_gate, we_up, we_down):
    logits = (x @ w_router).astype(jnp.float32)
    top_vals, top_idx = lax.top_k(logits, TOP_K)
    gates = jax.nn.softmax(top_vals, axis=-1)
    combine = jnp.einsum("bske,bsk->bse", jax.nn.one_hot(top_idx, N_EXPERTS, dtype=jnp.float32), gates)
    combine = combine.astype(x.dtype)
    out = jnp.zeros_like(x)
    for e in range(N_EXPERTS):
        out = out + combine[..., e:e + 1] * swiglu(x, we_gate[e], we_up[e], we_down[e])
    return out

def setup_inputs(seed: int = 0) -> dict:
    key = jax.random.key(seed)
    ks = jax.random.split(key, 24)
    n = jax.random.normal
    f32 = jnp.float32
    return {
        "x": n(ks[0], (BATCH, SEQ, D_MODEL), f32),
        "w_in": n(ks[1], (DEPTH, D_MODEL, IN_PROJ_WIDTH), f32) * D_MODEL ** -0.5,
        "conv_w": n(ks[2], (DEPTH, CONV_K, CONV_WIDTH), f32) * CONV_K ** -0.5,
        "v_g": 1.0 + 0.01 * n(ks[3], (DEPTH, GMLP_WIDTH), f32),
        "v_b": 0.01 * n(ks[4], (DEPTH, GMLP_WIDTH), f32),
        "w_s": n(ks[5], (DEPTH, GMLP_HEADS, CHUNK, CHUNK), f32) * CHUNK ** -0.5,
        "b_s": 1.0 + 0.01 * n(ks[6], (DEPTH, GMLP_HEADS, CHUNK), f32),
        "out_g": 1.0 + 0.01 * n(ks[7], (DEPTH, MIX_WIDTH), f32),
        "w_out": n(ks[8], (DEPTH, MIX_WIDTH, D_MODEL), f32) * (BETA * MIX_WIDTH ** -0.5),
        "ln1_g": 1.0 + 0.01 * n(ks[9], (DEPTH, D_MODEL), f32),
        "ln1_b": 0.01 * n(ks[10], (DEPTH, D_MODEL), f32),
        "ln2_g": 1.0 + 0.01 * n(ks[11], (DEPTH, D_MODEL), f32),
        "ln2_b": 0.01 * n(ks[12], (DEPTH, D_MODEL), f32),
        "w_gate": n(ks[13], (N_DENSE, D_MODEL, D_FF_DENSE), f32) * D_MODEL ** -0.5,
        "w_up": n(ks[14], (N_DENSE, D_MODEL, D_FF_DENSE), f32) * D_MODEL ** -0.5,
        "w_down": n(ks[15], (N_DENSE, D_FF_DENSE, D_MODEL), f32) * (BETA * D_FF_DENSE ** -0.5),
        "w_router": n(ks[16], (N_MOE, D_MODEL, N_EXPERTS), f32) * D_MODEL ** -0.5,
        "we_gate": n(ks[17], (N_MOE, N_EXPERTS, D_MODEL, D_FF_EXPERT), f32) * D_MODEL ** -0.5,
        "we_up": n(ks[18], (N_MOE, N_EXPERTS, D_MODEL, D_FF_EXPERT), f32) * D_MODEL ** -0.5,
        "we_down": n(ks[19], (N_MOE, N_EXPERTS, D_FF_EXPERT, D_MODEL), f32) * (BETA * D_FF_EXPERT ** -0.5),
    }

def reference(x, w_in, conv_w, v_g, v_b, w_s, b_s, out_g, w_out, ln1_g, ln1_b, ln2_g, ln2_b,
              w_gate, w_up, w_down, w_router, we_gate, we_up, we_down):
    for i in range(DEPTH):
        mix = hybrid_mixer(x, w_in[i], conv_w[i], v_g[i], v_b[i], w_s[i], b_s[i], out_g[i], w_out[i])
        x = layer_norm(ALPHA * x + mix, ln1_g[i], ln1_b[i])
        if i % 2 == 0:
            ffn = swiglu(x, w_gate[i // 2], w_up[i // 2], w_down[i // 2])
        else:
            ffn = moe_swiglu(x, w_router[i // 2], we_gate[i // 2], we_up[i // 2], we_down[i // 2])
        x = layer_norm(ALPHA * x + ffn, ln2_g[i], ln2_b[i])
    return x


_drawn_inputs = setup_inputs


def setup_inputs(seed=0):
    import zlib

    import numpy as np

    out = dict(_drawn_inputs(seed))
    spreads = {}
    factors = {'v_g': 8.0,
     'v_b': 8.0,
     'b_s': 8.0,
     'out_g': 8.0,
     'ln1_g': 3.076,
     'ln1_b': 2.963,
     'ln2_g': 3.458,
     'ln2_b': 3.134}
    for name, (base, spread) in spreads.items():
        noise = np.random.default_rng([zlib.crc32(name.encode()), seed]).standard_normal(out[name].shape)
        drawn = base * np.exp(spread * noise) if base else spread * noise
        out[name] = __import__('jax').numpy.asarray(drawn.astype(out[name].dtype))
    for name, factor in factors.items():
        out[name] = (out[name] * factor).astype(out[name].dtype)
    return out
```

```python
import concourse.bass as bass
from concourse import mybir
from contextlib import ExitStack

P = 128
BANK = 512
DEPTH = 2
ALPHA = (2 * DEPTH) ** 0.25
LN_EPS = 1e-5
RMS_EPS = 1e-6
TOP_K = 2


def hybrid_trunk_kernel(nc, x_in, w_in, conv_w, v_g, v_b, w_s, b_s, out_g, w_out, ln1_g, ln1_b, ln2_g, ln2_b,
                        w_gate, w_up, w_down, w_router, we_gate, we_up, we_down, out):
    f32 = mybir.dt.float32
    i32 = mybir.dt.int32
    ALU = mybir.AluOpType
    ACT = mybir.ActivationFunctionType
    X = mybir.AxisListType.X
    ds = bass.ds

    _, TOK, D = x_in.shape
    NT = TOK // P
    KD = D // P
    CW = conv_w.shape[2]
    TAPS = conv_w.shape[1]
    CB = CW // P
    GW = v_g.shape[1]
    HEADS = w_s.shape[1]
    E = we_gate.shape[1]
    FF_D = w_gate.shape[2]
    FF_E = we_gate.shape[3]
    CONV_HD = 64
    COL = 512
    RING = 7
    G2 = 2 * P
    MAIN = 96

    MIX_SLOTS = 5 + 2
    D_STEPS = FF_D // COL
    D_GROUPS = FF_D // G2
    DENSE_SLOTS = 3 * D_STEPS + 2
    MOE_BASE = 2 * MIX_SLOTS + DENSE_SLOTS
    E_STEPS = FF_E // COL
    E_GROUPS = FF_E // G2
    E_SLOTS = 3 * E_STEPS

    def slot_tiles(width):
        return [(a, min(P, width - a)) for a in range(0, width, P)]

    assert E_SLOTS % RING == 0 and E_GROUPS % 2 == 0 and MAIN <= P and FF_D == D_STEPS * COL + G2
    TURNS = E_SLOTS // RING

    ctx = ExitStack()
    with ctx:
        def sb(name, shape, dt=f32):
            return ctx.enter_context(nc.sbuf_tensor(name, shape, dt))

        def sem(name):
            return ctx.enter_context(nc.semaphore(name))

        ring = sb("ring", [P, RING, KD * COL])
        x = sb("x", [P, NT, D])
        xT = sb("xT", [P, KD, TOK])
        ln_rows = sb("ln_rows", [P, 4, D])
        v_rows = sb("v_rows", [P, 2, GW])
        bs_rows = sb("bs_rows", [P, DEPTH, HEADS, P])
        wsT = sb("wsT", [P, DEPTH * HEADS, P])
        work = sb("work", [P, 8452])
        h_buf = sb("h_buf", [P, 3, 2, TOK])
        silu_buf = sb("silu_buf", [P, 2, 2, TOK])
        ident = sb("ident", [P, P])
        mean_conv = sb("mean_conv", [P, P])
        mean_gmlp = sb("mean_gmlp", [P, P])
        before = sb("before", [P, P])
        ones = sb("ones", [P, P])
        N_CHAN = DEPTH * (TAPS * CB + 5 * KD)
        chan_rows = sb("chan_rows", [N_CHAN, P])
        chan = sb("chan", [P, N_CHAN])
        wr = sb("wr", [P, KD, E])
        slot_iota = sb("slot_iota", [P, TOK])
        rank = sb("rank", [P, NT, E])
        small = sb("small", [P, 256])
        eps_rms = sb("eps_rms", [P, 1])
        neg_half = sb("neg_half", [P, 1])
        count_i = sb("count_i", [1, E], i32)

        v = work[:, 0:1024].rearrange("p (n c) -> p n c", n=NT)
        cg = work[:, 1024:2048].rearrange("p (c t) -> p c t", c=CB)
        q = work[:, 2048:2048 + CB * (TOK + 2)].rearrange("p (c t) -> p c t", c=CB)
        conv = work[:, 3088:4112].rearrange("p (c t) -> p c t", c=CB)
        gu = work[:, 4112:5136].rearrange("p (c t) -> p c t", c=CB)
        zb = work[:, 5136:6160].rearrange("p (h n t) -> p h n t", h=HEADS, n=NT)
        zb2 = work[:, 5136:6160].rearrange("p (c t) -> p c t", c=CB)
        y = work[:, 6160:8208].rearrange("p (c t) -> p c t", c=KD)
        conv_sq, gmlp_sq = cg, work[:, 0:1024].rearrange("p (c t) -> p c t", c=CB)
        ws_raw = work[:, 6160:7184].rearrange("p (l s) -> p l s", s=P)
        xg = work[:, 0:2048].rearrange("p (k s) -> p k s", k=KD)
        yT = work[:, 2048:4096].rearrange("p (k s) -> p k s", k=KD)
        y_slots = work[:, 0:2048].rearrange("p (o d) -> p o d", o=NT)
        acc = work[:, 5120:7168].rearrange("p (n d) -> p n d", n=NT)
        pick = work[:, 7168:7680].rearrange("p (n s) -> p n s", n=NT)
        pickT = work[:, 7680:8192].rearrange("p (o t) -> p o t", o=NT)
        stats = small[:, 0:12]
        mv = small[:, 12:14]
        var_eps = small[:, 14:18]
        rstd = small[:, 18:22]
        logits = small[:, 32:48].rearrange("p (n e) -> p n e", n=NT)
        first_oh = small[:, 48:64].rearrange("p (n e) -> p n e", n=NT)
        second_oh = small[:, 64:80].rearrange("p (n e) -> p n e", n=NT)
        tmp_e = small[:, 80:96].rearrange("p (n e) -> p n e", n=NT)
        rest = small[:, 96:112].rearrange("p (n e) -> p n e", n=NT)
        combine = small[:, 112:128].rearrange("p (n e) -> p n e", n=NT)
        mask = small[:, 128:144].rearrange("p (n e) -> p n e", n=NT)
        slot_of = small[:, 144:162].rearrange("p (n e) -> p n e", n=NT)
        top = small[:, 164:166]
        top2 = small[:, 166:168]
        best = small[:, 168:170]
        gap = small[:, 170:172]
        exp_gap = small[:, 172:174]
        g_first = small[:, 174:176]
        g_second = small[:, 176:178]
        den = small[:, 178:180]

        O_G = DEPTH * TAPS * CB
        LN_C = [O_G + DEPTH * KD * (1 + i) for i in range(4)]

        def tap_col(l, k, c):
            i = (l * TAPS + k) * CB + c
            return chan[:, i:i + 1]

        def out_g_col(l, c):
            return chan[:, O_G + l * KD + c:O_G + l * KD + c + 1]

        def ln_col(which, l, k):
            i = LN_C[which] + l * KD + k
            return chan[:, i:i + 1]

        accp = ctx.enter_context(nc.psum_tensor("accp", [P, 4, BANK], f32))
        turn = ctx.enter_context(nc.psum_tensor("turn", [P, 4, BANK], f32))
        acc_half = accp[:, :, :].rearrange("p b (c s) -> p (b c) s", c=2)
        turn_half = turn[:, :, :].rearrange("p b (c s) -> p (b c) s", c=2)

        slot_filled = [sem(f"slot_filled{i}") for i in range(RING)]
        conv_rows_read, down_done = sem("conv_rows_read"), sem("down_done")
        x_loaded, ws_loaded, chan_loaded, vrows_loaded, bs_loaded, ln_loaded, wr_loaded = (
            sem(n) for n in ("x_loaded", "ws_loaded", "chan_loaded", "vrows_loaded", "bs_loaded", "ln_loaded",
                             "wr_loaded"))
        ln1_reloaded, ln2_reloaded, vrows_reloaded = sem("ln1_reloaded"), sem("ln2_reloaded"), sem("vrows_reloaded")
        ident_zero, ident_ready, consts_ready, before_ones, ws_masked, mean_conv_ready = (
            sem(n) for n in ("ident_zero", "ident_ready", "consts_ready", "before_ones", "ws_masked", "mean_conv_ready"))
        x_transposed, ws_transposed, chan_transposed = sem("x_transposed"), sem("ws_transposed"), sem("chan_transposed")
        wsT_ready, chan_ready = sem("wsT_ready"), sem("chan_ready")
        xT_lo, xT_hi = sem("xT_lo"), sem("xT_hi")
        v_proj, cg_proj, h_proj, z_done, bg_proj, u_proj = (
            sem(n) for n in ("v_proj", "cg_proj", "h_proj", "z_done", "bg_proj", "u_proj"))
        v_gelu, v_var, v_rstd, v_ready, cg_ready, q_ready, zb_ready, y_conv_raw = (
            sem(n) for n in ("v_gelu", "v_var", "v_rstd", "v_ready", "cg_ready", "q_ready", "zb_ready", "y_conv_raw"))
        u_gelu, y_gmlp_raw, conv_squared, gmlp_squared = (
            sem(n) for n in ("u_gelu", "y_gmlp_raw", "conv_squared", "gmlp_squared"))
        conv_mean, gmlp_mean, conv_rms, gmlp_rms, y_conv_ready, y_gmlp_ready = (
            sem(n) for n in ("conv_mean", "gmlp_mean", "conv_rms", "gmlp_rms", "y_conv_ready", "y_gmlp_ready"))
        sum_done, ln_var, ln_rstd, ln_norm, x_affine, affine_step = (
            sem(n) for n in ("sum_done", "ln_var", "ln_rstd", "ln_norm", "x_affine", "affine_step"))
        gu_done, silu_ready, h_ready = sem("gu_done"), sem("silu_ready"), sem("h_ready")
        logits_done, gap_ready, gap_exp, mask_ready, pos_done, counts_ready, pick_ready = (
            sem(n) for n in ("logits_done", "gap_ready", "gap_exp", "mask_ready", "pos_done", "counts_ready",
                             "pick_ready"))
        gathered, xg_lo, xg_hi, pick_transposed, pickT_ready = (
            sem(n) for n in ("gathered", "xg_lo", "xg_hi", "pick_transposed", "pickT_ready"))
        yT_lo, yT_hi, y_transposed, y_lo, y_hi, scattered, acc_added = (
            sem(n) for n in ("yT_lo", "yT_hi", "y_transposed", "y_lo", "y_hi", "scattered", "acc_added"))
        out_ready, out_written, dve_step = sem("out_ready"), sem("out_written"), sem("dve_step")

        def place(use):
            return use % RING, use // RING

        def cols(slot, width=COL, part=0):
            n = KD * width
            return ring[:, slot, part * n:(part + 1) * n].rearrange("p (k f) -> p k f", k=KD)

        def rows(slot, n=COL // P):
            return ring[:, slot, 0:n * D].rearrange("p (j d) -> p j d", j=n)

        block = ctx.enter_context(nc.Block())

        def mixer_reads(l):
            return [(v_proj, NT * (l + 1)), (cg_proj, 2 * (l + 1)), (h_proj, 2 * (l + 1)), (bg_proj, 2 * (l + 1)),
                    (u_proj, 2 * (l + 1)), (conv_rows_read, l + 1), (sum_done, NT * (2 * l + 1))]

        dense_reads = []
        for s in range(D_STEPS):
            dense_reads += [(gu_done, 2 * s + 2), (gu_done, 2 * s + 2), (down_done, 2 * s + 2)]
        dense_reads += [(gu_done, D_GROUPS), (sum_done, 2 * NT)]
        reads = mixer_reads(0) + dense_reads + mixer_reads(1)
        DOWN_BASE = D_GROUPS - 1

        @block.sync
        def _(sp):
            def fill(use, pairs):
                if use >= RING:
                    done, value = reads[use - RING]
                    sp.wait_ge(done, value)
                for dst, src in pairs:
                    sp.dma_start(dst, src).then_inc(slot_filled[use % RING], 16)

            def col_block(w, c0, width=COL):
                return w[:, c0:c0 + width].rearrange("(k p) f -> p k f", p=P)

            def row_block(w, r0, n=COL):
                return w[r0:r0 + n, :].rearrange("(j p) d -> p j d", p=P)

            W_IN_AT = [3 * CW + GW, CW, 2 * CW, 0, 3 * CW]
            for l in range(DEPTH):
                base = l * (MIX_SLOTS + DENSE_SLOTS)
                for i, c0 in enumerate(W_IN_AT):
                    fill(base + i, [(cols((base + i) % RING), col_block(w_in[l], c0))])
                for i in range(2):
                    use = base + 5 + i
                    fill(use, [(rows(use % RING), row_block(w_out[l], i * COL))])
                if l == 0:
                    for s in range(D_STEPS):
                        use = MIX_SLOTS + 3 * s
                        fill(use, [(cols(use % RING), col_block(w_gate[0], s * COL))])
                        fill(use + 1, [(cols((use + 1) % RING), col_block(w_up[0], s * COL))])
                        fill(use + 2, [(rows((use + 2) % RING), row_block(w_down[0], s * COL))])
                    use = MIX_SLOTS + 3 * D_STEPS
                    fill(use, [(cols(use % RING, G2, part), col_block(w[0], D_STEPS * COL, G2))
                               for part, w in enumerate((w_gate, w_up))])
                    fill(use + 1, [(rows((use + 1) % RING, 2), row_block(w_down[0], D_STEPS * COL, G2))])

            def fill_expert(e, i):
                s, kind = i // 3, i % 3
                slot = (MOE_BASE + i) % RING
                w = (we_gate, we_up, we_down)[kind]
                src = w[0, ds(e, 1)].rearrange("o (k p) f -> p (o k) f", p=P)
                if kind == 2:
                    src, dst = src[:, s * (COL // P):(s + 1) * (COL // P), :], rows(slot)
                else:
                    src, dst = src[:, :, s * COL:(s + 1) * COL], cols(slot)
                sp.dma_start(dst, src).then_inc(slot_filled[slot], 16)

            def wait_read(e, i):
                s, kind = i // 3, i % 3
                sp.wait_ge(down_done if kind == 2 else gu_done,
                           e * E_GROUPS + ((DOWN_BASE if kind == 2 else D_GROUPS) + 2 * s + 2))

            for i in range(RING):
                done, value = reads[MOE_BASE - RING + i]
                sp.wait_ge(done, value)
                fill_expert(0, i)
            with sp.Fori(0, E - 1) as e:
                for i in range(RING, E_SLOTS):
                    wait_read(e, i - RING)
                    fill_expert(e, i)
                for i in range(RING):
                    wait_read(e, E_SLOTS - RING + i)
                    fill_expert(e + 1, i)
            for i in range(RING, E_SLOTS):
                wait_read(E - 1, i - RING)
                fill_expert(E - 1, i)

            for n in range(NT):
                sp.wait_ge(out_ready, n + 1)
                sp.dma_start(out[0, n * P:(n + 1) * P, :], acc[:, n, :]).then_inc(out_written, 16)
            sp.wait_ge(out_written, 16 * NT)

        HALF_SLOT = place(MIX_SLOTS + 3 * D_STEPS)

        @block.gpsimd
        def _(pool):
            nc.gpsimd.memset(ident[:], 0.0).then_inc(ident_zero, 1)
            pool.wait_ge(ident_zero, 1)
            nc.gpsimd.affine_select(out=ident[:], in_=ident[:], compare_op=ALU.not_equal, fill=1.0, base=0,
                                    pattern=[[-1, P]], channel_multiplier=1).then_inc(ident_ready, 1)
            nc.gpsimd.memset(neg_half[:], -0.5)
            nc.gpsimd.memset(eps_rms[:], RMS_EPS)
            nc.gpsimd.memset(mean_gmlp[:], 1.0 / P)
            nc.gpsimd.memset(before[:], 1.0)
            nc.gpsimd.memset(ones[:], 1.0)
            nc.gpsimd.iota(slot_iota[:], pattern=[[1, TOK]], base=0, channel_multiplier=0,
                           allow_small_or_imprecise_dtypes=True)
            nc.gpsimd.iota(rank[:], pattern=[[0, NT], [-1, E]], base=E, channel_multiplier=0,
                           allow_small_or_imprecise_dtypes=True).then_inc(before_ones, 1)
            pool.wait_ge(before_ones, 1)
            nc.gpsimd.affine_select(out=before[:], in_=before[:], compare_op=ALU.is_gt, fill=0.0, base=0,
                                    pattern=[[1, P]], channel_multiplier=-1).then_inc(consts_ready, 1)
            pool.wait_ge(ws_loaded, 16)
            nc.gpsimd.affine_select(out=ws_raw, in_=ws_raw, compare_op=ALU.is_ge, fill=0.0, base=0,
                                    pattern=[[0, DEPTH * HEADS], [-1, P]], channel_multiplier=1).then_inc(ws_masked, 1)

            def power(var_sem, rstd_sem, at, n):
                pool.wait_ge(var_sem, n)
                nc.gpsimd.tensor_tensor(rstd[:, at:at + 1], var_eps[:, at:at + 1], neg_half[:],
                                        ALU.pow).then_inc(rstd_sem, 1)

            def affine(build, which):
                for n in range(NT):
                    pool.wait_ge(x_transposed, NT * build + n + 1)
                    at = 2 * (NT * (build - 1) + n)
                    nc.gpsimd.tensor_tensor(x[:, n, :], x[:, n, :], ln_rows[:, which, :],
                                            ALU.mult).then_inc(affine_step, 1)
                    pool.wait_ge(affine_step, at // 2 + 1)
                    nc.gpsimd.tensor_tensor(x[:, n, :], x[:, n, :], ln_rows[:, which + 1, :],
                                            ALU.add).then_inc(x_affine, 1)

            pool.wait_ge(ln_loaded, 16 * 4)
            for l in range(DEPTH):
                for n in range(NT):
                    power(v_var, v_rstd, n, NT * l + n + 1)
                if l == 0:
                    pool.wait_ge(v_ready, NT)
                    for i, a in enumerate((v_g, v_b)):
                        pool.dma_start(v_rows[:, i, :], a[1].partition_broadcast(P)).then_inc(vrows_reloaded, 16)
                for n in range(NT):
                    power(ln_var, ln_rstd, 2 + n, 2 * NT * l + n + 1)
                if l == 1:
                    pool.wait_ge(ln1_reloaded, 32)
                affine(2 * l + 1, 0)
                if l == 0:
                    pool.wait_ge(x_affine, NT)
                    for i, a in enumerate((ln1_g, ln1_b)):
                        pool.dma_start(ln_rows[:, i, :], a[1].partition_broadcast(P)).then_inc(ln1_reloaded, 16)
                    for n in range(NT):
                        power(ln_var, ln_rstd, 2 + n, NT + n + 1)
                    affine(2, 2)
                    pool.wait_ge(x_affine, 2 * NT)
                    for i, a in enumerate((ln2_g, ln2_b)):
                        pool.dma_start(ln_rows[:, 2 + i, :], a[1].partition_broadcast(P)).then_inc(ln2_reloaded, 16)
            for n in range(NT):
                power(ln_var, ln_rstd, 2 + n, 3 * NT + n + 1)

        @block.scalar
        def _(act):
            act.dma_start(x[:], x_in[0].rearrange("(n p) d -> p n d", p=P)).then_inc(x_loaded, 16)
            act.dma_start(ws_raw, w_s.rearrange("l h t s -> t (l h) s")).then_inc(ws_loaded, 16)
            r0 = 0
            for src in (conv_w.rearrange("l k (c p) -> (l k c) p", p=P),
                        *(a.rearrange("l (c p) -> (l c) p", p=P) for a in (out_g, ln1_g, ln1_b, ln2_g, ln2_b))):
                n = src.shape[0]
                act.dma_start(chan_rows[r0:r0 + n, :], src).then_inc(chan_loaded, 16)
                r0 += n
            for i, a in enumerate((v_g, v_b)):
                act.dma_start(v_rows[:, i, :], a[0].partition_broadcast(P)).then_inc(vrows_loaded, 16)
            act.dma_start(bs_rows[:], b_s.partition_broadcast(P)).then_inc(bs_loaded, 16)
            act.dma_start(wr[:], w_router[0].rearrange("(k p) e -> p k e", p=P)).then_inc(wr_loaded, 16)
            for i, a in enumerate((ln1_g, ln1_b, ln2_g, ln2_b)):
                act.dma_start(ln_rows[:, i, :], a[0].partition_broadcast(P)).then_inc(ln_loaded, 16)

            def xT_low_half(build, which=None, l=0):
                for n in range(NT):
                    act.wait_ge(x_transposed, NT * build + n + 1)
                    if which is None:
                        nc.scalar.copy(xT[:, 0:KD // 2, n * P:(n + 1) * P],
                                       turn[:, 2 * n, :].rearrange("p (k t) -> p k t", t=P)).then_inc(xT_lo, 1)
                        continue
                    for k in range(KD // 2):
                        last = nc.scalar.activation(xT[:, k, n * P:(n + 1) * P], turn[:, 2 * n, k * P:(k + 1) * P],
                                                    ACT.Identity, bias=ln_col(which + 1, l, k),
                                                    scale=ln_col(which, l, k))
                    last.then_inc(xT_lo, 1)

            def silu(j, width):
                return nc.scalar.activation(silu_buf[:, j % 2, :, 0:width],
                                            turn_half[:, 4 * (j % 2):4 * (j % 2) + 2, 0:width], ACT.Silu)

            xT_low_half(0)
            for l in range(DEPTH):
                for n in range(NT):
                    act.wait_ge(v_proj, NT * l + n + 1)
                    nc.scalar.activation(v[:, n, :], turn[:, n, :], ACT.Gelu).then_inc(v_gelu, 1)
                for i in range(2):
                    act.wait_ge(cg_proj, 2 * l + i + 1)
                    nc.scalar.copy(cg[:, 2 * i:2 * i + 2, :],
                                   turn_half[:, 4 + 2 * i:6 + 2 * i, :]).then_inc(cg_ready, 1)
                for i in range(2):
                    act.wait_ge(y_conv_raw, 2 * l + i + 1)
                    nc.scalar.activation(conv_sq[:, 2 * i:2 * i + 2, :], y[:, 2 * i:2 * i + 2, :],
                                         ACT.Square).then_inc(conv_squared, 1)
                for i in range(2):
                    act.wait_ge(u_proj, 2 * l + i + 1)
                    nc.scalar.activation(gu[:, 2 * i:2 * i + 2, :], turn_half[:, 2 * i:2 * i + 2, :],
                                         ACT.Gelu).then_inc(u_gelu, 1)
                for i in range(2):
                    act.wait_ge(y_gmlp_raw, 2 * l + i + 1)
                    nc.scalar.activation(gmlp_sq[:, 2 * i:2 * i + 2, :], y[:, CB + 2 * i:CB + 2 * i + 2, :],
                                         ACT.Square).then_inc(gmlp_squared, 1)
                act.wait_ge(consts_ready, 1)
                for i in range(2):
                    act.wait_ge(conv_mean, 2 * l + i + 1)
                    nc.scalar.activation(conv[:, 2 * i:2 * i + 2, :], turn_half[:, 4 + 2 * i:6 + 2 * i, :],
                                         ACT.Sqrt, bias=eps_rms[:]).then_inc(conv_rms, 1)
                for i in range(2):
                    act.wait_ge(gmlp_mean, 2 * l + i + 1)
                    nc.scalar.activation(zb2[:, 2 * i:2 * i + 2, :], turn_half[:, 2 * i:2 * i + 2, :],
                                         ACT.Sqrt, bias=eps_rms[:]).then_inc(gmlp_rms, 1)
                xT_low_half(2 * l + 1, 0, l)
                if l == 0:
                    for j in range(D_GROUPS):
                        act.wait_ge(gu_done, j + 1)
                        silu(j, TOK).then_inc(silu_ready, 1)
                    xT_low_half(2, 2, 0)
            act.wait_ge(gap_ready, 1)
            nc.scalar.activation(exp_gap, gap, ACT.Exp).then_inc(gap_exp, 1)

            act.wait_ge(counts_ready, 1)
            def expert(e, width):
                act.wait_ge(gathered, e * 2 + 1)
                nc.scalar.copy(xg[:, 0:KD // 2, 0:width], turn_half[:, 0:KD // 2, 0:width]).then_inc(xg_lo, 1)
                act.wait_ge(pick_transposed, e + 1)
                size = min(width, P)
                tiles = len(slot_tiles(width))
                nc.scalar.copy(pickT[0:size, 0:tiles, :], accp[0:size, 0:tiles, 0:TOK]).then_inc(pickT_ready, 1)
                for j in range(E_GROUPS):
                    act.wait_ge(gu_done, e * E_GROUPS + (D_GROUPS + j + 1))
                    silu(j, width).then_inc(silu_ready, 1)
                act.wait_ge(down_done, e * E_GROUPS + (DOWN_BASE + E_GROUPS))
                nc.scalar.copy(yT[:, 0:KD // 2, 0:width], acc_half[:, 0:KD // 2, 0:width]).then_inc(yT_lo, 1)
                act.wait_ge(y_transposed, e + 1)
                nc.scalar.copy(y_slots[0:size, 0:tiles, 0:BANK],
                               turn[0:size, 0:2 * tiles:2, :]).then_inc(y_lo, 1)

            with act.Fori(0, E) as e:
                many = act.value_load(count_i[0:1, ds(e, 1)], min_val=0, max_val=TOK)
                with act.If(many > MAIN):
                    expert(e, TOK)
                with act.Else():
                    expert(e, MAIN)

        @block.vector
        def _(dve):
            steps = [0]

            def step(ins):
                steps[0] += 1
                ins.then_inc(dve_step, 1)
                dve.wait_ge(dve_step, steps[0])

            def xT_high_half(build, which=None, l=0):
                for n in range(NT):
                    dve.wait_ge(x_transposed, NT * build + n + 1)
                    if which is None:
                        nc.vector.tensor_copy(xT[:, KD // 2:, n * P:(n + 1) * P],
                                              turn[:, 2 * n + 1, :].rearrange("p (k t) -> p k t", t=P)).then_inc(xT_hi, 1)
                        continue
                    for k in range(KD // 2, KD):
                        at = (k - KD // 2) * P
                        last = nc.vector.tensor_scalar(xT[:, k, n * P:(n + 1) * P], turn[:, 2 * n + 1, at:at + P],
                                                       ln_col(which, l, k), ln_col(which + 1, l, k), ALU.mult, ALU.add)
                    last.then_inc(xT_hi, 1)

            def statistics(rows_ap, at, width, eps, var_sem):
                for i in range(width // 512):
                    last = nc.vector.bn_stats(stats[:, 6 * i:6 * i + 6], rows_ap[:, i * 512:(i + 1) * 512])
                step(last)
                step(nc.vector.bn_aggr(mv, stats[:, 0:6 * (width // 512)]))
                nc.vector.tensor_scalar_add(var_eps[:, at:at + 1], mv[:, 1:2], eps).then_inc(var_sem, 1)

            def layer_norm_tile(number, n):
                dve.wait_ge(sum_done, NT * number + n + 1)
                if number:
                    dve.wait_ge(x_affine, NT * (number - 1) + n + 1)
                step(nc.vector.scalar_tensor_tensor(out=x[:, n, :], in0=x[:, n, :], scalar=ALPHA,
                                                    in1=accp[:, 2 * n:2 * n + 2, :].rearrange("p b c -> p (b c)"),
                                                    op0=ALU.mult, op1=ALU.add))
                statistics(x[:, n, :], 2 + n, D, LN_EPS, ln_var)
                dve.wait_ge(ln_rstd, NT * number + n + 1)
                nc.vector.tensor_scalar(x[:, n, :], x[:, n, :], mv[:, 0:1], rstd[:, 2 + n:3 + n],
                                        ALU.subtract, ALU.mult).then_inc(ln_norm, 1)

            def gate_times_up(j, width):
                return nc.vector.tensor_tensor(h_buf[:, j % 3, :, 0:width],
                                               turn_half[:, 4 * (j % 2) + 2:4 * (j % 2) + 4, 0:width],
                                               silu_buf[:, j % 2, :, 0:width], ALU.mult)

            def choose(e):
                for n in range(NT):
                    last = nc.vector.tensor_scalar(pick[:, n, :], slot_iota[:], slot_of[:, n, ds(e, 1)], None,
                                                   ALU.is_equal)
                last.then_inc(pick_ready, 1)

            nc.vector.memset(q[:, :, 0:2], 0.0)
            step(nc.vector.memset(mean_conv[:], 0.0))
            for h in range(P // CONV_HD):
                a = h * CONV_HD
                last = nc.vector.memset(mean_conv[a:a + CONV_HD, a:a + CONV_HD], 1.0 / CONV_HD)
            last.then_inc(mean_conv_ready, 1)
            xT_high_half(0)
            dve.wait_ge(chan_transposed, 1)
            nc.vector.tensor_copy(chan[:], accp[:, 3, 0:N_CHAN]).then_inc(chan_ready, 1)
            dve.wait_ge(ws_transposed, 1)
            nc.vector.tensor_copy(wsT[:], accp[:, 0:2, :].rearrange("p b (l s) -> p (b l) s", s=P)).then_inc(wsT_ready, 1)
            dve.wait_ge(chan_ready, 1)
            dve.wait_ge(bs_loaded, 16)
            dve.wait_ge(vrows_loaded, 32)

            for l in range(DEPTH):
                for n in range(NT):
                    dve.wait_ge(v_gelu, NT * l + n + 1)
                    statistics(v[:, n, :], n, GW, LN_EPS, v_var)
                    dve.wait_ge(v_rstd, NT * l + n + 1)
                    step(nc.vector.tensor_scalar(v[:, n, :], v[:, n, :], mv[:, 0:1], rstd[:, n:n + 1],
                                                 ALU.subtract, ALU.mult))
                    if l == 1 and n == 0:
                        dve.wait_ge(vrows_reloaded, 32)
                    step(nc.vector.tensor_tensor(v[:, n, :], v[:, n, :], v_rows[:, 0, :], ALU.mult))
                    nc.vector.tensor_tensor(v[:, n, :], v[:, n, :], v_rows[:, 1, :], ALU.add).then_inc(v_ready, 1)
                for i in range(2):
                    dve.wait_ge(cg_ready, 2 * l + i + 1)
                    dve.wait_ge(h_proj, 2 * l + i + 1)
                    nc.vector.tensor_tensor(q[:, 2 * i:2 * i + 2, 2:], turn_half[:, 2 * i:2 * i + 2, :],
                                            cg[:, 2 * i:2 * i + 2, :], ALU.mult).then_inc(q_ready, 1)
                dve.wait_ge(q_ready, 2 * l + 2)
                dve.wait_ge(z_done, l + 1)
                for i in range(2):
                    for n in range(NT):
                        last = nc.vector.tensor_tensor(zb[:, 2 * i:2 * i + 2, n, :],
                                                       acc_half[:, 2 * i:2 * i + 2, n * P:(n + 1) * P],
                                                       bs_rows[:, l, 2 * i:2 * i + 2, :], ALU.add)
                last.then_inc(zb_ready, 1)
                for c in range(CB):
                    last = nc.vector.tensor_scalar(conv[:, c, :], q[:, c, 0:TOK], tap_col(l, 0, c), None, ALU.mult)
                step(last)
                for k in range(1, TAPS):
                    for c in range(CB):
                        last = nc.vector.scalar_tensor_tensor(out=conv[:, c, :], in0=q[:, c, k:k + TOK],
                                                              scalar=tap_col(l, k, c), in1=conv[:, c, :],
                                                              op0=ALU.mult, op1=ALU.add)
                    step(last)
                for i in range(2):
                    dve.wait_ge(bg_proj, 2 * l + i + 1)
                    nc.vector.tensor_tensor(y[:, 2 * i:2 * i + 2, :], turn_half[:, 4 + 2 * i:6 + 2 * i, :],
                                            conv[:, 2 * i:2 * i + 2, :], ALU.mult).then_inc(y_conv_raw, 1)
                dve.wait_ge(zb_ready, l + 1)
                for i in range(2):
                    dve.wait_ge(u_gelu, 2 * l + i + 1)
                    nc.vector.tensor_tensor(y[:, CB + 2 * i:CB + 2 * i + 2, :], gu[:, 2 * i:2 * i + 2, :],
                                            zb2[:, 2 * i:2 * i + 2, :], ALU.mult).then_inc(y_gmlp_raw, 1)
                for rms_sem, buf, c0, ready in ((conv_rms, conv, 0, y_conv_ready), (gmlp_rms, zb2, CB, y_gmlp_ready)):
                    for i in range(2):
                        dve.wait_ge(rms_sem, 2 * l + i + 1)
                        step(nc.vector.reciprocal(buf[:, 2 * i:2 * i + 2, :], buf[:, 2 * i:2 * i + 2, :]))
                        for c in (2 * i, 2 * i + 1):
                            last = nc.vector.scalar_tensor_tensor(out=y[:, c0 + c, :], in0=y[:, c0 + c, :],
                                                                  scalar=out_g_col(l, c0 + c), in1=buf[:, c, :],
                                                                  op0=ALU.mult, op1=ALU.mult)
                        last.then_inc(ready, 1)
                if l == 0:
                    dve.wait_ge(x_transposed, NT)
                for n in range(NT):
                    layer_norm_tile(2 * l, n)
                xT_high_half(2 * l + 1, 0, l)
                if l == 0:
                    for j in range(D_GROUPS):
                        dve.wait_ge(silu_ready, j + 1)
                        gate_times_up(j, TOK).then_inc(h_ready, 1)
                    for n in range(NT):
                        layer_norm_tile(1, n)
                    xT_high_half(2, 2, 0)

            def bcast(a):
                return a.unsqueeze(2).to_broadcast([P, NT, E])

            dve.wait_ge(logits_done, 1)
            step(nc.vector.tensor_copy(logits, accp[:, 0, 0:NT * E].rearrange("p (n e) -> p n e", n=NT)))
            for values, peak, chosen in ((logits, top, first_oh), (rest, top2, second_oh)):
                if values is rest:
                    step(nc.vector.scalar_tensor_tensor(out=rest, in0=first_oh, scalar=-3.0e38, in1=logits,
                                                        op0=ALU.mult, op1=ALU.add))
                step(nc.vector.tensor_reduce(peak, values, X, ALU.max))
                step(nc.vector.tensor_tensor(tmp_e, values, bcast(peak), ALU.is_equal))
                step(nc.vector.tensor_tensor(tmp_e, tmp_e, rank[:], ALU.mult))
                step(nc.vector.tensor_reduce(best, tmp_e, X, ALU.max))
                step(nc.vector.tensor_tensor(chosen, tmp_e, bcast(best), ALU.is_equal))
            nc.vector.tensor_tensor(mask, first_oh, second_oh, ALU.add).then_inc(mask_ready, 1)
            nc.vector.tensor_tensor(gap, top2, top, ALU.subtract).then_inc(gap_ready, 1)
            dve.wait_ge(gap_exp, 1)
            step(nc.vector.tensor_scalar_add(den, exp_gap, 1.0))
            step(nc.vector.reciprocal(g_first, den))
            step(nc.vector.tensor_tensor(g_second, exp_gap, g_first, ALU.mult))
            nc.vector.tensor_tensor(combine, first_oh, bcast(g_first), ALU.mult)
            step(nc.vector.tensor_tensor(tmp_e, second_oh, bcast(g_second), ALU.mult))
            step(nc.vector.tensor_tensor(combine, combine, tmp_e, ALU.add))
            dve.wait_ge(pos_done, 1)
            nc.vector.tensor_copy(count_i[:], accp[0:1, 1, NT * E:(NT + 1) * E]).then_inc(counts_ready, 1)
            nc.vector.memset(slot_of[:, :, E:E + 1], -1000.0)
            step(nc.vector.scalar_tensor_tensor(out=slot_of[:, :, 0:E],
                                                in0=accp[:, 1, 0:NT * E].rearrange("p (n e) -> p n e", n=NT),
                                                scalar=1000.0, in1=mask, op0=ALU.add, op1=ALU.mult))
            step(nc.vector.tensor_scalar_add(slot_of[:, :, 0:E], slot_of[:, :, 0:E], -1000.0))
            choose(0)
            for n in range(NT):
                dve.wait_ge(x_affine, NT * 2 + n + 1)
                nc.vector.tensor_scalar(acc[:, n, :], x[:, n, :], ALPHA, None, ALU.mult).then_inc(acc_added, 1)

            dve.wait_ge(counts_ready, 1)
            def expert(e, width):
                dve.wait_ge(gathered, e * 2 + 2)
                nc.vector.tensor_copy(xg[:, KD // 2:, 0:width], turn_half[:, KD // 2:, 0:width]).then_inc(xg_hi, 1)
                for j in range(E_GROUPS):
                    dve.wait_ge(silu_ready, e * E_GROUPS + (D_GROUPS + j + 1))
                    gate_times_up(j, width).then_inc(h_ready, 1)
                    if j == 0:
                        choose(e + 1)
                dve.wait_ge(down_done, e * E_GROUPS + (DOWN_BASE + E_GROUPS))
                nc.vector.tensor_copy(yT[:, KD // 2:, 0:width], acc_half[:, KD // 2:, 0:width]).then_inc(yT_hi, 1)
                dve.wait_ge(y_transposed, e + 1)
                size = min(width, P)
                tiles = len(slot_tiles(width))
                nc.vector.tensor_copy(y_slots[0:size, 0:tiles, BANK:],
                                      turn[0:size, 1:2 * tiles:2, :]).then_inc(y_hi, 1)
                dve.wait_ge(acc_added, e * NT + NT)
                for n in range(NT):
                    dve.wait_ge(scattered, e * NT + n + 1)
                    nc.vector.scalar_tensor_tensor(out=acc[:, n, :],
                                                   in0=accp[:, 2 * n:2 * n + 2, :].rearrange("p b c -> p (b c)"),
                                                   scalar=combine[:, n, ds(e, 1)], in1=acc[:, n, :],
                                                   op0=ALU.mult, op1=ALU.add).then_inc(acc_added, 1)

            with dve.Fori(0, E) as e:
                many = dve.value_load(count_i[0:1, ds(e, 1)], min_val=0, max_val=TOK)
                with dve.If(many > MAIN):
                    expert(e, TOK)
                with dve.Else():
                    expert(e, MAIN)

            dve.wait_ge(acc_added, NT * (E + 1))
            dve.wait_ge(ln2_reloaded, 32)
            for n in range(NT):
                statistics(acc[:, n, :], 2 + n, D, LN_EPS, ln_var)
                dve.wait_ge(ln_rstd, NT * 3 + n + 1)
                step(nc.vector.tensor_scalar(acc[:, n, :], acc[:, n, :], mv[:, 0:1], rstd[:, 2 + n:3 + n],
                                             ALU.subtract, ALU.mult))
                step(nc.vector.tensor_tensor(acc[:, n, :], acc[:, n, :], ln_rows[:, 2, :], ALU.mult))
                nc.vector.tensor_tensor(acc[:, n, :], acc[:, n, :], ln_rows[:, 3, :], ALU.add).then_inc(out_ready, 1)

        @block.tensor
        def _(pe):
            def arrived(use, dmas=1):
                slot, turn_no = place(use)
                extra = 1 if slot == HALF_SLOT[0] and turn_no >= HALF_SLOT[1] else 0
                pe.wait_ge(slot_filled[slot], 16 * (turn_no + 1 + extra))
                return slot

            def transpose_x(build):
                for n in range(NT):
                    if build:
                        pe.wait_ge(ln_norm, NT * (build - 1) + n + 1)
                    for k in range(KD):
                        last = nc.tensor.transpose(turn[:, 2 * n + k // 4, (k % 4) * P:(k % 4 + 1) * P],
                                                   x[:, n, k * P:(k + 1) * P], ident[:])
                    last.then_inc(x_transposed, 1)

            def project(weights, bank0, done_sem):
                for c in range(CB):
                    for k in range(KD):
                        last = nc.tensor.matmul(turn_half[:, bank0 * 2 + c, :], weights[:, k, c * P:(c + 1) * P],
                                                xT[:, k, :], start=(k == 0), stop=(k == KD - 1))
                    if c % 2:
                        last.then_inc(done_sem, 1)

            def gate_up(j, wg, wu, rhs, width, f0):
                for half, w in enumerate((wg, wu)):
                    for b in range(2):
                        for k in range(KD):
                            last = nc.tensor.matmul(turn_half[:, 4 * (j % 2) + 2 * half + b, 0:width],
                                                    w[:, k, f0 + b * P:f0 + (b + 1) * P], rhs[:, k, 0:width],
                                                    start=(k == 0), stop=(k == KD - 1))
                return last

            pe.wait_ge(ident_ready, 1)
            pe.wait_ge(x_loaded, 16)
            transpose_x(0)
            pe.wait_ge(chan_loaded, 16 * 6)
            nc.tensor.transpose(accp[:, 3, 0:N_CHAN], chan_rows[:], ident[0:N_CHAN, 0:N_CHAN]).then_inc(chan_transposed, 1)
            pe.wait_ge(ws_masked, 1)
            for i in range(DEPTH * HEADS):
                last = nc.tensor.transpose(accp[:, i // 4, (i % 4) * P:(i % 4 + 1) * P], ws_raw[:, i, :], ident[:])
            last.then_inc(ws_transposed, 1)
            pe.wait_ge(consts_ready, 1)
            pe.wait_ge(mean_conv_ready, 1)

            for l in range(DEPTH):
                base = l * (MIX_SLOTS + DENSE_SLOTS)
                slot = arrived(base)
                for n in range(NT):
                    pe.wait_ge(xT_lo, NT * 2 * l + n + 1)
                    pe.wait_ge(xT_hi, NT * 2 * l + n + 1)
                    for k in range(KD):
                        last = nc.tensor.matmul(turn[:, n, :], xT[:, k, n * P:(n + 1) * P], cols(slot)[:, k, :],
                                                start=(k == 0), stop=(k == KD - 1))
                    last.then_inc(v_proj, 1)
                slot = arrived(base + 1)
                project(cols(slot), 2, cg_proj)
                slot = arrived(base + 2)
                pe.wait_ge(v_gelu, NT * (l + 1))
                project(cols(slot), 0, h_proj)
                pe.wait_ge(v_ready, NT * (l + 1))
                if l == 0:
                    pe.wait_ge(wsT_ready, 1)
                for h in range(HEADS):
                    for n in range(NT):
                        last = nc.tensor.matmul(acc_half[:, h, n * P:(n + 1) * P], v[:, n, h * P:(h + 1) * P],
                                                wsT[:, l * HEADS + h, :], start=True, stop=True)
                last.then_inc(z_done, 1)
                slot = arrived(base + 3)
                pe.wait_ge(cg_ready, 2 * (l + 1))
                project(cols(slot), 2, bg_proj)
                slot = arrived(base + 4)
                pe.wait_ge(q_ready, 2 * (l + 1))
                project(cols(slot), 0, u_proj)
                for i in range(2):
                    pe.wait_ge(conv_squared, 2 * l + i + 1)
                    nc.tensor.matmul(turn[:, 2 + i, :], mean_conv[:], conv_sq[:, 2 * i:2 * i + 2, :].rearrange(
                        "p c t -> p (c t)"), start=True, stop=True).then_inc(conv_mean, 1)
                slot = arrived(base + 5)
                pe.wait_ge(zb_ready, l + 1)
                pe.wait_ge(y_conv_ready, 2 * (l + 1))
                for n in range(NT):
                    if n == 1:
                        for i in range(2):
                            pe.wait_ge(gmlp_squared, 2 * l + i + 1)
                            nc.tensor.matmul(turn[:, i, :], mean_gmlp[:], gmlp_sq[:, 2 * i:2 * i + 2, :].rearrange(
                                "p c t -> p (c t)"), start=True, stop=True).then_inc(gmlp_mean, 1)
                    for half in range(2):
                        for k in range(CB):
                            last = nc.tensor.matmul(accp[:, 2 * n + half, :], y[:, k, n * P:(n + 1) * P],
                                                    rows(slot)[:, k, half * BANK:(half + 1) * BANK],
                                                    start=(k == 0), stop=False)
                last.then_inc(conv_rows_read, 1)
                slot = arrived(base + 6)
                pe.wait_ge(y_gmlp_ready, 2 * (l + 1))
                for n in range(NT):
                    for half in range(2):
                        for k in range(HEADS):
                            last = nc.tensor.matmul(accp[:, 2 * n + half, :], y[:, CB + k, n * P:(n + 1) * P],
                                                    rows(slot)[:, k, half * BANK:(half + 1) * BANK],
                                                    start=False, stop=(k == HEADS - 1))
                    last.then_inc(sum_done, 1)
                transpose_x(2 * l + 1)
                for n in range(NT):
                    pe.wait_ge(xT_lo, NT * (2 * l + 1) + n + 1)
                    pe.wait_ge(xT_hi, NT * (2 * l + 1) + n + 1)
                if l == 1:
                    break

                def down(j):
                    s = j // 2
                    slot = arrived(MIX_SLOTS + 3 * s + (2 if s < D_STEPS else 1))
                    pe.wait_ge(h_ready, j + 1)
                    for b in range(2):
                        for n in range(NT):
                            for half in range(2):
                                last = nc.tensor.matmul(accp[:, 2 * n + half, :], h_buf[:, j % 3, b, n * P:(n + 1) * P],
                                                        rows(slot)[:, 2 * (j % 2) + b, half * BANK:(half + 1) * BANK],
                                                        start=(j == 0 and b == 0), stop=(j == D_GROUPS - 1 and b == 1))
                            if j == D_GROUPS - 1 and b == 1:
                                last.then_inc(sum_done, 1)
                    if j < D_GROUPS - 1:
                        last.then_inc(down_done, 1)

                for j in range(D_GROUPS):
                    s = j // 2
                    if j >= 2:
                        pe.wait_ge(h_ready, j - 1)
                    if s < D_STEPS:
                        gs = arrived(MIX_SLOTS + 3 * s)
                        us = arrived(MIX_SLOTS + 3 * s + 1)
                        last = gate_up(j, cols(gs), cols(us), xT, TOK, (j % 2) * G2)
                    else:
                        gs = arrived(MIX_SLOTS + 3 * s)
                        last = gate_up(j, cols(gs, G2, 0), cols(gs, G2, 1), xT, TOK, 0)
                    last.then_inc(gu_done, 1)
                    if j >= 2:
                        down(j - 2)
                down(D_GROUPS - 2)
                down(D_GROUPS - 1)
                transpose_x(2)

            pe.wait_ge(wr_loaded, 16)
            for n in range(NT):
                for k in range(KD):
                    last = nc.tensor.matmul(accp[:, 0, n * E:(n + 1) * E], xT[:, k, n * P:(n + 1) * P], wr[:, k, :],
                                            start=(k == 0), stop=(k == KD - 1))
            last.then_inc(logits_done, 1)
            pe.wait_ge(mask_ready, 1)
            nc.tensor.matmul(accp[:, 1, 0:E], before[:], mask[:, 0, :], start=True, stop=True)
            nc.tensor.matmul(accp[:, 1, E:2 * E], before[:], mask[:, 1, :], start=True, stop=False)
            nc.tensor.matmul(accp[:, 1, E:2 * E], ones[:], mask[:, 0, :], start=False, stop=True)
            nc.tensor.matmul(accp[:, 1, 2 * E:3 * E], ones[:], mask[:, 0, :], start=True, stop=False)
            nc.tensor.matmul(accp[:, 1, 2 * E:3 * E], ones[:], mask[:, 1, :], start=False, stop=True).then_inc(pos_done, 1)

            pe.wait_ge(counts_ready, 1)
            pe.wait_ge(x_affine, NT * 3)
            def expert(e, width):
                tiles = slot_tiles(width)

                def arrived_e(i):
                    slot, turn_no = place(MOE_BASE + i)
                    extra = 1 if slot == HALF_SLOT[0] else 0
                    pe.wait_ge(slot_filled[slot], e * (16 * TURNS) + 16 * (turn_no + 1 + extra))

                def gather(k0, k1):
                    for k in range(k0, k1):
                        for n in range(NT):
                            last = nc.tensor.matmul(turn_half[:, k, 0:width], x[:, n, k * P:(k + 1) * P],
                                                    pick[:, n, 0:width], start=(n == 0), stop=(n == NT - 1))
                    return last

                def down(j):
                    slot = place(MOE_BASE + 3 * (j // 2) + 2)[0]
                    for b in range(2):
                        for k in range(KD):
                            last = nc.tensor.matmul(acc_half[:, k, 0:width],
                                                    rows(slot)[:, 2 * (j % 2) + b, k * P:(k + 1) * P],
                                                    h_buf[:, j % 3, b, 0:width],
                                                    start=(j == 0 and b == 0 and k % 2 == 0),
                                                    stop=(j == E_GROUPS - 1 and b == 1), skip_group_check=True)
                    last.then_inc(down_done, 1)

                pe.wait_ge(pick_ready, e + 1)
                gather(0, KD // 2).then_inc(gathered, 1)
                gather(KD // 2, KD).then_inc(gathered, 1)
                pe.wait_ge(acc_added, e * NT + NT)
                for o, (a, size) in enumerate(tiles):
                    for n in range(NT):
                        last = nc.tensor.transpose(accp[0:size, o, n * P:(n + 1) * P], pick[:, n, a:a + size], ident[:])
                last.then_inc(pick_transposed, 1)

                for j in range(E_GROUPS + 2):
                    if j == 0:
                        pe.wait_ge(xg_lo, e + 1)
                        pe.wait_ge(xg_hi, e + 1)
                    if j == 2:
                        pe.wait_ge(pickT_ready, e + 1)
                    if j >= 2:
                        pe.wait_ge(h_ready, e * E_GROUPS + (D_GROUPS + j - 1))
                    if j < E_GROUPS:
                        step = 3 * (j // 2)
                        if j % 2 == 0:
                            arrived_e(step)
                            arrived_e(step + 1)
                        gate_up(j, cols((MOE_BASE + step) % RING), cols((MOE_BASE + step + 1) % RING), xg, width,
                                (j % 2) * G2).then_inc(gu_done, 1)
                    if j >= 2:
                        if j % 2 == 0:
                            arrived_e(3 * (j // 2 - 1) + 2)
                        down(j - 2)

                pe.wait_ge(yT_lo, e + 1)
                pe.wait_ge(yT_hi, e + 1)
                for o, (a, size) in enumerate(tiles):
                    for k in range(KD):
                        last = nc.tensor.transpose(turn[0:size, 2 * o + k // 4, (k % 4) * P:(k % 4 + 1) * P],
                                                   yT[:, k, a:a + size], ident[:])
                last.then_inc(y_transposed, 1)
                pe.wait_ge(y_lo, e + 1)
                pe.wait_ge(y_hi, e + 1)
                for n in range(NT):
                    for half in range(2):
                        for o, (a, size) in enumerate(tiles):
                            last = nc.tensor.matmul(accp[:, 2 * n + half, :], pickT[0:size, o, n * P:(n + 1) * P],
                                                    y_slots[0:size, o, half * BANK:(half + 1) * BANK],
                                                    start=(o == 0), stop=(o == len(tiles) - 1))
                    last.then_inc(scattered, 1)

            with pe.Fori(0, E) as e:
                many = pe.value_load(count_i[0:1, ds(e, 1)], min_val=0, max_val=TOK)
                with pe.If(many > MAIN):
                    expert(e, TOK)
                with pe.Else():
                    expert(e, MAIN)


_INS = ["x", "w_in", "conv_w", "v_g", "v_b", "w_s", "b_s", "out_g", "w_out", "ln1_g", "ln1_b", "ln2_g", "ln2_b",
        "w_gate", "w_up", "w_down", "w_router", "we_gate", "we_up", "we_down"]


def kernel(**inputs):
    import numpy as np
    import concourse.bacc as bacc
    from concourse.bass_utils import run_bass_kernel_spmd

    nc = bacc.Bacc("TRN2", target_bir_lowering=False, num_devices=1)
    arrays, args = {}, []
    for name in _INS:
        a = np.ascontiguousarray(inputs[name])
        arrays[f"in_{name}"] = a
        args.append(nc.dram_tensor(f"in_{name}", a.shape, mybir.dt.from_np(a.dtype), kind="ExternalInput").ap())
    shape = arrays["in_x"].shape
    out = nc.dram_tensor("out_x", shape, mybir.dt.float32, kind="ExternalOutput").ap()
    hybrid_trunk_kernel(nc, *args, out)
    r = run_bass_kernel_spmd(nc, [arrays], core_ids=[0])
    return r.results[0]["out_x"]
```

```python
import concourse.bass as bass
from concourse import mybir
from contextlib import ExitStack

P = 128
BANK = 512
DEPTH = 2
ALPHA = (2 * DEPTH) ** 0.25
LN_EPS = 1e-5
RMS_EPS = 1e-6
TOP_K = 2


def hybrid_trunk_kernel(nc, x_in, w_in, conv_w, v_g, v_b, w_s, b_s, out_g, w_out, ln1_g, ln1_b, ln2_g, ln2_b,
                        w_gate, w_up, w_down, w_router, we_gate, we_up, we_down, out):
    f32 = mybir.dt.float32
    f32r = mybir.dt.float32r
    i32 = mybir.dt.int32
    ALU = mybir.AluOpType
    ACT = mybir.ActivationFunctionType
    X = mybir.AxisListType.X
    ds = bass.ds

    _, TOK, D = x_in.shape
    NT = TOK // P
    KD = D // P
    CW = conv_w.shape[2]
    TAPS = conv_w.shape[1]
    CB = CW // P
    GW = v_g.shape[1]
    HEADS = w_s.shape[1]
    E = we_gate.shape[1]
    FF_D = w_gate.shape[2]
    FF_E = we_gate.shape[3]
    CONV_HD = 64

    PIECE = 2048
    RING = 7
    PARTS = 3
    HALF = 2 * P
    COL = 512
    MIX = 2 * 5 + 4
    GROUPS = FF_D // HALF
    STEPS = FF_E // COL
    E_PIECES = 6 * STEPS
    DENSE_AT = MIX
    MIX1_AT = DENSE_AT + 3 * GROUPS
    MOE_AT = MIX1_AT + MIX
    assert E_PIECES % RING == 0 and E_PIECES % PARTS == 0 and FF_D % HALF == 0 and FF_E % COL == 0
    TURNS = E_PIECES // RING

    def dense_gate(j):
        return DENSE_AT + (3 * j - 1 if j else 0)

    def dense_up(j):
        return dense_gate(j) + 1

    def dense_down(j):
        return dense_gate(j + 1) + 2 if j < GROUPS - 1 else MIX1_AT - 1

    def step_at(s):
        return 6 * s - 2 if s else 0

    def step_down(s):
        return step_at(s + 1) + 4 if s < STEPS - 1 else E_PIECES - 2

    ctx = ExitStack()
    with ctx:
        def sb(name, shape, dt=f32):
            return ctx.enter_context(nc.sbuf_tensor(name, shape, dt))

        def sem(name):
            return ctx.enter_context(nc.semaphore(name))

        raw = sb("raw", [P, RING, PIECE])
        w_hi = sb("w_hi", [P, PARTS, PIECE], f32r)
        w_lo = sb("w_lo", [P, PARTS, PIECE], f32r)
        x = sb("x", [P, NT, D])
        t_hi = sb("t_hi", [P, KD * TOK], f32r)
        t_lo = sb("t_lo", [P, KD * TOK], f32r)
        a_hi = sb("a_hi", [P, KD * TOK], f32r)
        a_lo = sb("a_lo", [P, KD * TOK], f32r)
        hT_hi = sb("hT_hi", [P, 4 * TOK], f32r)
        hT_lo = sb("hT_lo", [P, 4 * TOK], f32r)
        pick = sb("pick", [P, NT, TOK], f32r)
        pickT = sb("pickT", [P, NT, TOK], f32r)
        ln_rows = sb("ln_rows", [P, 2, D])
        v_rows = sb("v_rows", [P, 2, GW])
        bs_rows = sb("bs_rows", [P, DEPTH, HEADS, P])
        wsT = sb("wsT", [P, DEPTH * HEADS, P])
        work = sb("work", [P, 6160])
        ident = sb("ident", [P, P])
        mean_conv = sb("mean_conv", [P, P])
        mean_gmlp = sb("mean_gmlp", [P, P])
        before = sb("before", [P, P])
        ones = sb("ones", [P, P])
        N_CHAN = DEPTH * (TAPS * CB + 5 * KD)
        chan_rows = sb("chan_rows", [N_CHAN, P])
        chan = sb("chan", [P, N_CHAN])
        wr = sb("wr", [P, KD, E])
        slot_iota = sb("slot_iota", [P, TOK])
        rank = sb("rank", [P, NT, E])
        small = sb("small", [P, 208])
        eps_rms = sb("eps_rms", [P, 1])
        neg_half = sb("neg_half", [P, 1])
        count_i = sb("count_i", [1, E], i32)

        v = work[:, 0:1024].rearrange("p (n c) -> p n c", n=NT)
        gmlp_sq = work[:, 0:1024].rearrange("p (c t) -> p c t", c=CB)
        cg = work[:, 1024:2048].rearrange("p (c t) -> p c t", c=CB)
        conv = cg
        q = work[:, 2048:3080].rearrange("p (c t) -> p c t", c=CB)
        conv_sq = work[:, 2048:3072].rearrange("p (c t) -> p c t", c=CB)
        zb = work[:, 3088:4112].rearrange("p (h n t) -> p h n t", h=HEADS, n=NT)
        zb2 = work[:, 3088:4112].rearrange("p (c t) -> p c t", c=CB)
        y = work[:, 4112:6160].rearrange("p (c t) -> p c t", c=KD)
        ws_raw = work[:, 4112:5136].rearrange("p (l s) -> p l s", s=P)
        silu_buf = work[:, 4112:5136].rearrange("p (i c t) -> p i c t", i=2, c=2)
        h_buf = work[:, 5136:6160].rearrange("p (i c t) -> p i c t", i=2, c=2)
        silu_e = work[:, 4112:5136].rearrange("p (i f) -> p i f", i=2)
        h_e = work[:, 5136:6160].rearrange("p (i f) -> p i f", i=2)
        xT = work[:, 0:2048].rearrange("p (k t) -> p k t", k=KD)
        xT_hi, xT_lo, y_hi, y_lo, xg_hi, xg_lo = (
            a[:, :].rearrange("p (k t) -> p k t", k=KD) for a in (t_hi, t_lo, a_hi, a_lo, a_hi, a_lo))
        x_hi, x_lo, ys_hi, ys_lo = (
            a[:, :].rearrange("p (n d) -> p n d", n=NT) for a in (t_hi, t_lo, a_hi, a_lo))
        h_hi, h_lo = (a[:, 0:4 * TOK].rearrange("p (i b t) -> p i b t", i=2, b=2) for a in (a_hi, a_lo))
        stats = small[:, 0:12]
        mv = [small[:, 12:14], small[:, 14:16]]
        var_eps = small[:, 16:20]
        rstd = small[:, 20:24]
        shift = small[:, 24:26]
        logits = small[:, 32:48].rearrange("p (n e) -> p n e", n=NT)
        first_oh = small[:, 48:64].rearrange("p (n e) -> p n e", n=NT)
        second_oh = small[:, 64:80].rearrange("p (n e) -> p n e", n=NT)
        tmp_e = small[:, 80:96].rearrange("p (n e) -> p n e", n=NT)
        rest = small[:, 96:112].rearrange("p (n e) -> p n e", n=NT)
        combine = small[:, 112:128].rearrange("p (n e) -> p n e", n=NT)
        mask = small[:, 128:144].rearrange("p (n e) -> p n e", n=NT)
        slot_of = small[:, 144:162].rearrange("p (n e) -> p n e", n=NT)
        top = small[:, 164:166]
        top2 = small[:, 166:168]
        best = small[:, 168:170]
        gap = small[:, 170:172]
        exp_gap = small[:, 172:174]
        g_first = small[:, 174:176]
        g_second = small[:, 176:178]
        den = small[:, 178:180]

        O_G = DEPTH * TAPS * CB
        LN_C = [O_G + DEPTH * KD * (1 + i) for i in range(4)]

        def tap_col(l, k, c):
            i = (l * TAPS + k) * CB + c
            return chan[:, i:i + 1]

        def out_g_col(l, c):
            return chan[:, O_G + l * KD + c:O_G + l * KD + c + 1]

        def ln_col(which, l, k):
            i = LN_C[which] + l * KD + k
            return chan[:, i:i + 1]

        accp = ctx.enter_context(nc.psum_tensor("accp", [P, 4, BANK], f32))
        turn = ctx.enter_context(nc.psum_tensor("turn", [P, 4, BANK], f32))
        acc_half = accp[:, :, :].rearrange("p b (c s) -> p (b c) s", c=2)
        turn_half = turn[:, :, :].rearrange("p b (c s) -> p (b c) s", c=2)

        def tile_sum(n):
            return accp[:, 2 * n:2 * n + 2, :].rearrange("p b c -> p (b c)")

        slot_filled = [sem(f"slot_filled{i}") for i in range(RING)]
        xT_low, xT_high = sem("xT_low"), sem("xT_high")
        vrows_reloaded, ln_reloaded = sem("vrows_reloaded"), sem("ln_reloaded")
        hi_done, split_done, piece_used = sem("hi_done"), sem("split_done"), sem("piece_used")
        x_loaded, ws_loaded, chan_loaded, vrows_loaded, bs_loaded, ln_loaded, wr_loaded = (
            sem(n) for n in ("x_loaded", "ws_loaded", "chan_loaded", "vrows_loaded", "bs_loaded", "ln_loaded",
                             "wr_loaded"))
        ident_zero, ident_ready, consts_ready, before_ones, ws_masked, mean_conv_ready = (
            sem(n) for n in ("ident_zero", "ident_ready", "consts_ready", "before_ones", "ws_masked",
                             "mean_conv_ready"))
        x_transposed, ws_transposed, chan_transposed = sem("x_transposed"), sem("ws_transposed"), sem("chan_transposed")
        wsT_ready, chan_ready, xT_hi_ready, xT_ready = (
            sem(n) for n in ("wsT_ready", "chan_ready", "xT_hi_ready", "xT_ready"))
        z_done, v_gelu, v_var, v_rstd, v_ready, cg_ready, q_ready, zb_ready, y_conv_raw = (
            sem(n) for n in ("z_done", "v_gelu", "v_var", "v_rstd", "v_ready", "cg_ready", "q_ready", "zb_ready",
                             "y_conv_raw"))
        u_gelu, y_gmlp_raw, conv_squared, gmlp_squared = (
            sem(n) for n in ("u_gelu", "y_gmlp_raw", "conv_squared", "gmlp_squared"))
        conv_mean, gmlp_mean, rms_log, rms_ready, y_normed, y_hi_ready, y_ready = (
            sem(n) for n in ("conv_mean", "gmlp_mean", "rms_log", "rms_ready", "y_normed", "y_hi_ready", "y_ready"))
        sum_done, ln_var, ln_rstd, ln_coef, ln_norm, x_affine, affine_step = (
            sem(n) for n in ("sum_done", "ln_var", "ln_rstd", "ln_coef", "ln_norm", "x_affine", "affine_step"))
        silu_ready, h_whole, h_hi_ready, h_ready = (sem(n) for n in ("silu_ready", "h_whole", "h_hi_ready", "h_ready"))
        logits_done, gap_ready, gap_exp, mask_ready, pos_done, counts_ready, pick_ready, x_hi_ready, x_lo_ready = (
            sem(n) for n in ("logits_done", "gap_ready", "gap_exp", "mask_ready", "pos_done", "counts_ready",
                             "pick_ready", "x_hi_ready", "x_lo_ready"))
        gathered, xg_hi_ready, xg_lo_ready, pick_transposed, pickT_ready = (
            sem(n) for n in ("gathered", "xg_hi_ready", "xg_lo_ready", "pick_transposed", "pickT_ready"))
        e_silu, e_h, e_hT, e_hT_hi, e_hT_lo, ys_hi_ready, ys_ready, scattered, acc_added = (
            sem(n) for n in ("e_silu", "e_h", "e_hT", "e_hT_hi", "e_hT_lo", "ys_hi_ready", "ys_ready", "scattered",
                             "acc_added"))
        out_ready, out_written, dve_step = sem("out_ready"), sem("out_written"), sem("dve_step")

        def upto(p, e=0):
            return e * E_PIECES + (p + 1)

        block = ctx.enter_context(nc.Block())

        @block.sync
        def _(sp):
            def load(p, src, e=0):
                if p >= RING:
                    sp.wait_ge(split_done, upto(p - RING, e))
                dst = raw[:, p % RING, :].rearrange("p (k f) -> p k f", k=src.shape[1])
                sp.dma_start(dst, src).then_inc(slot_filled[p % RING], 16)

            def columns(w, c0):
                return w[:, c0:c0 + HALF].rearrange("(k p) f -> p k f", p=P)

            def rows(w, r0):
                return w[r0:r0 + HALF, :].rearrange("(j p) d -> p j d", p=P)

            def mixer(at, l, between):
                for i, c0 in enumerate((3 * CW + GW, CW, 2 * CW, 0, 3 * CW)):
                    for half in range(2):
                        load(at + 2 * i + half, columns(w_in[l], c0 + half * HALF))
                    between(i)
                for i in range(4):
                    load(at + 10 + i, rows(w_out[l], i * HALF))

            def small_inputs(i):
                if i == 0:
                    for j, a in enumerate((v_g, v_b)):
                        sp.dma_start(v_rows[:, j, :], a[0].partition_broadcast(P)).then_inc(vrows_loaded, 16)
                if i == 2:
                    sp.dma_start(bs_rows[:], b_s.partition_broadcast(P)).then_inc(bs_loaded, 16)
                if i == 4:
                    for j, a in enumerate((ln1_g, ln1_b)):
                        sp.dma_start(ln_rows[:, j, :], a[0].partition_broadcast(P)).then_inc(ln_loaded, 16)
                    sp.dma_start(wr[:], w_router[0].rearrange("(k p) e -> p k e", p=P)).then_inc(wr_loaded, 16)

            mixer(0, 0, small_inputs)
            for j in range(GROUPS):
                load(dense_gate(j), columns(w_gate[0], j * HALF))
                load(dense_up(j), columns(w_up[0], j * HALF))
                if j:
                    load(dense_down(j - 1), rows(w_down[0], (j - 1) * HALF))
            load(dense_down(GROUPS - 1), rows(w_down[0], (GROUPS - 1) * HALF))
            mixer(MIX1_AT, 1, lambda i: None)

            with sp.Fori(0, E) as e:
                wg, wu, wd = (w[0, ds(e, 1)].rearrange("o (k p) f -> p (o k) f", p=P) for w in (we_gate, we_up, we_down))
                for s in range(STEPS + 1):
                    if s < STEPS:
                        for i, w in enumerate((wg, wu)):
                            for half in range(2):
                                load(MOE_AT + step_at(s) + 2 * i + half,
                                     w[:, half * KD // 2:(half + 1) * KD // 2, s * COL:(s + 1) * COL], e)
                    if s:
                        for half in range(2):
                            j0 = 4 * (s - 1) + 2 * half
                            load(MOE_AT + step_down(s - 1) + half, wd[:, j0:j0 + 2, :], e)

            for n in range(NT):
                sp.wait_ge(out_ready, n + 1)
                sp.dma_start(out[0, n * P:(n + 1) * P, :], x[:, n, :]).then_inc(out_written, 16)
            sp.wait_ge(out_written, 16 * NT)

        @block.gpsimd
        def _(pool):
            nc.gpsimd.memset(ident[:], 0.0).then_inc(ident_zero, 1)
            pool.wait_ge(ident_zero, 1)
            nc.gpsimd.affine_select(out=ident[:], in_=ident[:], compare_op=ALU.not_equal, fill=1.0, base=0,
                                    pattern=[[-1, P]], channel_multiplier=1).then_inc(ident_ready, 1)
            nc.gpsimd.memset(neg_half[:], -0.5)
            nc.gpsimd.memset(eps_rms[:], RMS_EPS)
            nc.gpsimd.memset(mean_gmlp[:], 1.0 / P)
            nc.gpsimd.memset(before[:], 1.0)
            nc.gpsimd.memset(ones[:], 1.0)
            nc.gpsimd.iota(slot_iota[:], pattern=[[1, TOK]], base=0, channel_multiplier=0,
                           allow_small_or_imprecise_dtypes=True)
            nc.gpsimd.iota(rank[:], pattern=[[0, NT], [-1, E]], base=E, channel_multiplier=0,
                           allow_small_or_imprecise_dtypes=True).then_inc(before_ones, 1)
            pool.wait_ge(before_ones, 1)
            nc.gpsimd.affine_select(out=before[:], in_=before[:], compare_op=ALU.is_gt, fill=0.0, base=0,
                                    pattern=[[1, P]], channel_multiplier=-1).then_inc(consts_ready, 1)
            pool.wait_ge(ws_loaded, 16)
            nc.gpsimd.affine_select(out=ws_raw, in_=ws_raw, compare_op=ALU.is_ge, fill=0.0, base=0,
                                    pattern=[[0, DEPTH * HEADS], [-1, P]], channel_multiplier=1).then_inc(ws_masked, 1)

            def power(var_sem, rstd_sem, at, n):
                pool.wait_ge(var_sem, n)
                nc.gpsimd.tensor_tensor(rstd[:, at:at + 1], var_eps[:, at:at + 1], neg_half[:],
                                        ALU.pow).then_inc(rstd_sem, 1)

            def layer_norm(number, following):
                for n in range(NT):
                    power(ln_var, ln_rstd, 2 + n, NT * number + n + 1)
                pool.wait_ge(*((ln_reloaded, 32 * number) if number else (ln_loaded, 32)))
                for n in range(NT):
                    pool.wait_ge(x_transposed, NT * (number + 1) + n + 1)
                    nc.gpsimd.tensor_tensor(x[:, n, :], x[:, n, :], ln_rows[:, 0, :],
                                            ALU.mult).then_inc(affine_step, 1)
                    pool.wait_ge(affine_step, NT * number + n + 1)
                    nc.gpsimd.tensor_tensor(x[:, n, :], x[:, n, :], ln_rows[:, 1, :], ALU.add).then_inc(x_affine, 1)
                pool.wait_ge(x_affine, NT * (number + 1))
                for i, a in enumerate(following):
                    pool.dma_start(ln_rows[:, i, :], a.partition_broadcast(P)).then_inc(ln_reloaded, 16)

            for l in range(DEPTH):
                for n in range(NT):
                    power(v_var, v_rstd, n, NT * l + n + 1)
                if l == 0:
                    pool.wait_ge(v_ready, NT)
                    for i, a in enumerate((v_g, v_b)):
                        pool.dma_start(v_rows[:, i, :], a[1].partition_broadcast(P)).then_inc(vrows_reloaded, 16)
                    layer_norm(0, (ln2_g[0], ln2_b[0]))
                    layer_norm(1, (ln1_g[1], ln1_b[1]))
                else:
                    layer_norm(2, (ln2_g[1], ln2_b[1]))
            for n in range(NT):
                power(ln_var, ln_rstd, 2 + n, 3 * NT + n + 1)

        @block.scalar
        def _(act):
            act.dma_start(x[:], x_in[0].rearrange("(n p) d -> p n d", p=P)).then_inc(x_loaded, 16)
            act.dma_start(ws_raw, w_s.rearrange("l h t s -> t (l h) s")).then_inc(ws_loaded, 16)
            r0 = 0
            for src in (conv_w.rearrange("l k (c p) -> (l k c) p", p=P),
                        *(a.rearrange("l (c p) -> (l c) p", p=P) for a in (out_g, ln1_g, ln1_b, ln2_g, ln2_b))):
                n = src.shape[0]
                act.dma_start(chan_rows[r0:r0 + n, :], src).then_inc(chan_loaded, 16)
                r0 += n

            def split_hi(p, e=0):
                act.wait_ge(slot_filled[p % RING], e * (16 * TURNS) + 16 * (p // RING + 1))
                if p >= PARTS:
                    act.wait_ge(piece_used, upto(p - PARTS, e))
                nc.scalar.copy(w_hi[:, p % PARTS, :], raw[:, p % RING, :]).then_inc(hi_done, 1)

            def splits(first, last, e=0):
                for p in range(first, last + 1):
                    split_hi(p, e)

            def used(p, e=0):
                act.wait_ge(piece_used, upto(p, e))

            def transposed_hi(build, which=None, l=0):
                for n in range(NT):
                    act.wait_ge(x_transposed, NT * build + n + 1)
                    at = slice(n * P, (n + 1) * P)
                    if which is None:
                        nc.scalar.copy(xT_hi[:, :, at], turn[:, 2 * n:2 * n + 2, :].rearrange(
                            "p b (k t) -> p (b k) t", t=P)).then_inc(xT_hi_ready, 1)
                        continue
                    for k in range(KD // 2):
                        last = nc.scalar.activation(xT[:, k, at], turn[:, 2 * n, k * P:(k + 1) * P], ACT.Identity,
                                                    bias=ln_col(which + 1, l, k), scale=ln_col(which, l, k))
                    last.then_inc(xT_low, 1)
                    if build < 3:
                        at_n = NT * (build - 1) + n + 1
                        act.wait_ge(xT_low, at_n)
                        act.wait_ge(xT_high, at_n)
                        nc.scalar.copy(xT_hi[:, :, at], xT[:, :, at]).then_inc(xT_hi_ready, 1)

            def normalise(number):
                for n in range(NT):
                    act.wait_ge(ln_coef, NT * number + n + 1)
                    nc.scalar.activation(x[:, n, :], x[:, n, :], ACT.Identity, bias=shift[:, n:n + 1],
                                         scale=rstd[:, 2 + n:3 + n]).then_inc(ln_norm, 1)

            transposed_hi(0)
            splits(0, 2)
            act.wait_ge(chan_ready, 1)
            act.wait_ge(consts_ready, 1)
            for l in range(DEPTH):
                at = l * MIX1_AT
                for n in range(NT):
                    used(at + 1)
                    nc.scalar.activation(v[:, n, :], turn[:, n, :], ACT.Gelu).then_inc(v_gelu, 1)
                splits(at + 3, at + 4)
                for i in range(2):
                    used(at + 2 + i)
                    nc.scalar.copy(cg[:, 2 * i:2 * i + 2, :],
                                   turn_half[:, 4 + 2 * i:6 + 2 * i, :]).then_inc(cg_ready, 1)
                    split_hi(at + 5 + i)
                splits(at + 7, at + 10)
                for i in range(2):
                    act.wait_ge(y_conv_raw, 2 * l + i + 1)
                    nc.scalar.activation(conv_sq[:, 2 * i:2 * i + 2, :], y[:, 2 * i:2 * i + 2, :],
                                         ACT.Square).then_inc(conv_squared, 1)
                for i in range(2):
                    split_hi(at + 11 + i)
                    used(at + 8 + i)
                    nc.scalar.activation(y[:, CB + 2 * i:CB + 2 * i + 2, :], turn_half[:, 2 * i:2 * i + 2, :],
                                         ACT.Gelu).then_inc(u_gelu, 1)

                def roots(group, mean_sem, banks, buf):
                    for i in range(2):
                        act.wait_ge(mean_sem, 2 * l + i + 1)
                        nc.scalar.activation(buf[:, 2 * i:2 * i + 2, :], turn_half[:, banks + 2 * i:banks + 2 * i + 2, :],
                                             ACT.Ln, bias=eps_rms[:]).then_inc(rms_log, 1)
                    for i in range(2):
                        act.wait_ge(rms_log, 4 * l + 2 * group + i + 1)
                        nc.scalar.activation(buf[:, 2 * i:2 * i + 2, :], buf[:, 2 * i:2 * i + 2, :], ACT.Exp,
                                             scale=-0.5).then_inc(rms_ready, 1)

                def round_y(group):
                    act.wait_ge(y_normed, 2 * l + group + 1)
                    nc.scalar.copy(y_hi[:, CB * group:CB * (group + 1), :],
                                   y[:, CB * group:CB * (group + 1), :]).then_inc(y_hi_ready, 1)

                for i in range(2):
                    act.wait_ge(y_gmlp_raw, 2 * l + i + 1)
                    nc.scalar.activation(gmlp_sq[:, 2 * i:2 * i + 2, :], y[:, CB + 2 * i:CB + 2 * i + 2, :],
                                         ACT.Square).then_inc(gmlp_squared, 1)
                roots(0, conv_mean, 4, conv)
                round_y(0)
                split_hi(at + 13)
                roots(1, gmlp_mean, 0, zb2)
                round_y(1)
                if l == 0:
                    splits(at + 14, at + 16)
                    normalise(0)
                    transposed_hi(1, 0, 0)
                    for j in range(GROUPS):
                        if 0 < j < GROUPS - 1:
                            split_hi(dense_gate(j + 1))
                        used(dense_up(j))
                        nc.scalar.activation(silu_buf[:, j % 2], turn_half[:, 4 * (j % 2):4 * (j % 2) + 2, :],
                                             ACT.Silu).then_inc(silu_ready, 1)
                        if 0 < j < GROUPS - 1:
                            split_hi(dense_up(j + 1))
                        if j == 0:
                            split_hi(dense_up(1))
                        act.wait_ge(h_whole, j + 1)
                        nc.scalar.copy(h_hi[:, j % 2], h_buf[:, j % 2]).then_inc(h_hi_ready, 1)
                        split_hi(dense_down(j))
                    splits(MIX1_AT, MIX1_AT + 2)
                    normalise(1)
                    transposed_hi(2, 2, 0)
                else:
                    normalise(2)
                    transposed_hi(3, 0, 1)

            act.wait_ge(gap_ready, 1)
            nc.scalar.activation(exp_gap, gap, ACT.Exp).then_inc(gap_exp, 1)
            for n in range(NT):
                act.wait_ge(x_affine, NT * 2 + n + 1)
                nc.scalar.copy(x_hi[:, n, :], x[:, n, :]).then_inc(x_hi_ready, 1)

            act.wait_ge(counts_ready, 1)

            def expert(e, tiles):
                def split_e(first, last):
                    splits(MOE_AT + first, MOE_AT + last, e)

                def silu_step(s):
                    used(MOE_AT + step_at(s) + 1, e)
                    if tiles == 1:
                        nc.scalar.activation(silu_e[:, s % 2, :], turn[:, 2 * (s % 2), :],
                                             ACT.Silu).then_inc(e_silu, 1)
                    else:
                        nc.scalar.activation(silu_e, turn[:, 0:4:2, :], ACT.Silu).then_inc(e_silu, 1)

                def round_h(s):
                    act.wait_ge(e_hT, e * STEPS + (s + 1))
                    if tiles == 1:
                        nc.scalar.copy(hT_hi[:, (s % 2) * BANK:(s % 2 + 1) * BANK],
                                       accp[:, 2 + s % 2, :]).then_inc(e_hT_hi, 1)
                    else:
                        nc.scalar.copy(hT_hi[:, :].rearrange("p (o f) -> p o f", o=2),
                                       turn[:, 0:4:2, :]).then_inc(e_hT_hi, 1)

                split_e(0, 0)
                act.wait_ge(gathered, e * 2 + 1)
                nc.scalar.copy(xg_hi[:, :, 0:tiles * P], (turn_half if tiles == 2 else turn[:, 0:2, :].rearrange(
                    "p b (k t) -> p (b k) t", t=P))).then_inc(xg_hi_ready, 1)
                act.wait_ge(pick_transposed, e + 1)
                nc.scalar.copy(pickT[:, 0:tiles, :], accp[:, 2, 0:tiles * TOK].rearrange(
                    "p (o t) -> p o t", o=tiles)).then_inc(pickT_ready, 1)
                split_e(1, 3)
                silu_step(0)
                if tiles == 2:
                    round_h(0)
                for s in range(1, STEPS):
                    b = step_at(s)
                    split_e(b, b + 3)
                    silu_step(s)
                    if tiles == 1:
                        round_h(s - 1)
                    split_e(b + 4, b + 5)
                    if tiles == 2:
                        round_h(s)
                split_e(E_PIECES - 2, E_PIECES - 1)
                if tiles == 1:
                    round_h(STEPS - 1)
                used(MOE_AT + E_PIECES - 1, e)
                nc.scalar.copy(ys_hi[:, 0:tiles, :], accp[:, 0:2 * tiles, :].rearrange(
                    "p (o b) c -> p o (b c)", o=tiles)).then_inc(ys_hi_ready, 1)

            with act.Fori(0, E) as e:
                many = act.value_load(count_i[0:1, ds(e, 1)], min_val=0, max_val=TOK)
                with act.If(many > P):
                    expert(e, 2)
                with act.Else():
                    expert(e, 1)

        @block.vector
        def _(dve):
            steps = [0]

            def step(ins):
                steps[0] += 1
                ins.then_inc(dve_step, 1)
                dve.wait_ge(dve_step, steps[0])

            def rest_of(out, whole, hi):
                return nc.vector.tensor_tensor(out, whole, hi.bitcast(f32), ALU.subtract)

            def split_lo(p, e=0):
                dve.wait_ge(hi_done, upto(p, e))
                rest_of(w_lo[:, p % PARTS, :], raw[:, p % RING, :], w_hi[:, p % PARTS, :]).then_inc(split_done, 1)

            def splits(first, last, e=0):
                for p in range(first, last + 1):
                    split_lo(p, e)

            def used(p, e=0):
                dve.wait_ge(piece_used, upto(p, e))

            def transposed_rest(build, which=None, l=0):
                for n in range(NT):
                    dve.wait_ge(x_transposed, NT * build + n + 1)
                    at = slice(n * P, (n + 1) * P)
                    if which is None:
                        dve.wait_ge(xT_hi_ready, NT * build + n + 1)
                        rest_of(xT_lo[:, :, at], turn[:, 2 * n:2 * n + 2, :].rearrange("p b (k t) -> p (b k) t", t=P),
                                xT_hi[:, :, at]).then_inc(xT_ready, 1)
                        continue
                    for k in range(KD // 2, KD):
                        k4 = k - KD // 2
                        last = nc.vector.tensor_scalar(xT[:, k, at], turn[:, 2 * n + 1, k4 * P:(k4 + 1) * P],
                                                       ln_col(which, l, k), ln_col(which + 1, l, k), ALU.mult, ALU.add)
                    last.then_inc(xT_high, 1)
                for n in range(NT):
                    at = slice(n * P, (n + 1) * P)
                    if which is None or build == 3:
                        continue
                    dve.wait_ge(xT_hi_ready, NT * build + n + 1)
                    rest_of(xT_lo[:, :, at], xT[:, :, at], xT_hi[:, :, at]).then_inc(xT_ready, 1)

            def statistics(rows_ap, n, at, width, eps, var_sem):
                for i in range(width // 512):
                    last = nc.vector.bn_stats(stats[:, 6 * i:6 * i + 6], rows_ap[:, i * 512:(i + 1) * 512])
                step(last)
                step(nc.vector.bn_aggr(mv[n], stats[:, 0:6 * (width // 512)]))
                nc.vector.tensor_scalar_add(var_eps[:, at:at + 1], mv[n][:, 1:2], eps).then_inc(var_sem, 1)

            def coefficients(number, n):
                dve.wait_ge(ln_rstd, NT * number + n + 1)
                nc.vector.scalar_tensor_tensor(out=shift[:, n:n + 1], in0=mv[n][:, 0:1], scalar=-1.0,
                                               in1=rstd[:, 2 + n:3 + n], op0=ALU.mult, op1=ALU.mult).then_inc(ln_coef, 1)

            def layer_norm(number, last_piece):
                for n in range(NT):
                    if n == 0:
                        dve.wait_ge(sum_done, number + 1)
                    else:
                        used(last_piece)
                    if number:
                        dve.wait_ge(x_affine, NT * (number - 1) + n + 1)
                    step(nc.vector.scalar_tensor_tensor(out=x[:, n, :], in0=x[:, n, :], scalar=ALPHA, in1=tile_sum(n),
                                                        op0=ALU.mult, op1=ALU.add))
                    if n:
                        coefficients(number, n - 1)
                    statistics(x[:, n, :], n, 2 + n, D, LN_EPS, ln_var)
                coefficients(number, NT - 1)

            def choose(e):
                for n in range(NT):
                    last = nc.vector.tensor_scalar(pick[:, n, :], slot_iota[:], slot_of[:, n, ds(e, 1)], None,
                                                   ALU.is_equal)
                last.then_inc(pick_ready, 1)

            step(nc.vector.memset(mean_conv[:], 0.0))
            for h in range(P // CONV_HD):
                a = h * CONV_HD
                last = nc.vector.memset(mean_conv[a:a + CONV_HD, a:a + CONV_HD], 1.0 / CONV_HD)
            last.then_inc(mean_conv_ready, 1)
            transposed_rest(0)
            splits(0, 2)
            dve.wait_ge(chan_transposed, 1)
            nc.vector.tensor_copy(chan[:], accp[:, 3, 0:N_CHAN]).then_inc(chan_ready, 1)
            dve.wait_ge(ws_transposed, 1)
            nc.vector.tensor_copy(wsT[:], accp[:, 0:2, :].rearrange("p b (l s) -> p (b l) s", s=P)).then_inc(wsT_ready, 1)
            dve.wait_ge(chan_ready, 1)

            for l in range(DEPTH):
                at = l * MIX1_AT
                step(nc.vector.memset(q[:, :, 0:TAPS - 1], 0.0))
                split_lo(at + 3)
                dve.wait_ge(vrows_reloaded if l else vrows_loaded, 32)
                for n in range(NT):
                    dve.wait_ge(v_gelu, NT * l + n + 1)
                    statistics(v[:, n, :], n, n, GW, LN_EPS, v_var)
                    dve.wait_ge(v_rstd, NT * l + n + 1)
                    step(nc.vector.tensor_scalar(v[:, n, :], v[:, n, :], mv[n][:, 0:1], rstd[:, n:n + 1],
                                                 ALU.subtract, ALU.mult))
                    step(nc.vector.tensor_tensor(v[:, n, :], v[:, n, :], v_rows[:, 0, :], ALU.mult))
                    nc.vector.tensor_tensor(v[:, n, :], v[:, n, :], v_rows[:, 1, :], ALU.add).then_inc(v_ready, 1)
                    split_lo(at + 4 + n)
                splits(at + 6, at + 7)
                for i in range(2):
                    dve.wait_ge(cg_ready, 2 * l + i + 1)
                    used(at + 4 + i)
                    nc.vector.tensor_tensor(q[:, 2 * i:2 * i + 2, 2:], turn_half[:, 2 * i:2 * i + 2, :],
                                            cg[:, 2 * i:2 * i + 2, :], ALU.mult).then_inc(q_ready, 1)
                split_lo(at + 8)
                dve.wait_ge(q_ready, 2 * l + 2)
                dve.wait_ge(bs_loaded, 16)
                dve.wait_ge(z_done, l + 1)
                for i in range(2):
                    for n in range(NT):
                        last = nc.vector.tensor_tensor(zb[:, 2 * i:2 * i + 2, n, :],
                                                       acc_half[:, 2 * i:2 * i + 2, n * P:(n + 1) * P],
                                                       bs_rows[:, l, 2 * i:2 * i + 2, :], ALU.add)
                last.then_inc(zb_ready, 1)
                for c in range(CB):
                    last = nc.vector.tensor_scalar(conv[:, c, :], q[:, c, 0:TOK], tap_col(l, 0, c), None, ALU.mult)
                step(last)
                for k in range(1, TAPS):
                    for c in range(CB):
                        last = nc.vector.scalar_tensor_tensor(out=conv[:, c, :], in0=q[:, c, k:k + TOK],
                                                              scalar=tap_col(l, k, c), in1=conv[:, c, :],
                                                              op0=ALU.mult, op1=ALU.add)
                    step(last)
                for i in range(2):
                    split_lo(at + 9 + i)
                    used(at + 6 + i)
                    nc.vector.tensor_tensor(y[:, 2 * i:2 * i + 2, :], turn_half[:, 4 + 2 * i:6 + 2 * i, :],
                                            conv[:, 2 * i:2 * i + 2, :], ALU.mult).then_inc(y_conv_raw, 1)
                dve.wait_ge(y_conv_raw, 2 * l + 2)
                dve.wait_ge(zb_ready, l + 1)
                for i in range(2):
                    split_lo(at + 11 + i)
                    dve.wait_ge(u_gelu, 2 * l + i + 1)
                    nc.vector.tensor_tensor(y[:, CB + 2 * i:CB + 2 * i + 2, :], y[:, CB + 2 * i:CB + 2 * i + 2, :],
                                            zb2[:, 2 * i:2 * i + 2, :], ALU.mult).then_inc(y_gmlp_raw, 1)
                dve.wait_ge(y_gmlp_raw, 2 * l + 2)

                def over_rms(group, buf):
                    c0 = CB * group
                    for i in range(2):
                        dve.wait_ge(rms_ready, 4 * l + 2 * group + i + 1)
                        for c in (2 * i, 2 * i + 1):
                            last = nc.vector.scalar_tensor_tensor(out=y[:, c0 + c, :], in0=y[:, c0 + c, :],
                                                                  scalar=out_g_col(l, c0 + c), in1=buf[:, c, :],
                                                                  op0=ALU.mult, op1=ALU.mult)
                    last.then_inc(y_normed, 1)
                    dve.wait_ge(y_hi_ready, 2 * l + group + 1)
                    rest_of(y_lo[:, c0:c0 + CB, :], y[:, c0:c0 + CB, :], y_hi[:, c0:c0 + CB, :]).then_inc(y_ready, 1)

                over_rms(0, conv)
                split_lo(at + 13)
                over_rms(1, zb2)
                if l == 0:
                    splits(at + 14, at + 16)
                    layer_norm(0, at + 13)
                    transposed_rest(1, 0, 0)
                    for j in range(GROUPS):
                        if 0 < j < GROUPS - 1:
                            split_lo(dense_gate(j + 1))
                        dve.wait_ge(silu_ready, j + 1)
                        nc.vector.tensor_tensor(h_buf[:, j % 2], turn_half[:, 4 * (j % 2) + 2:4 * (j % 2) + 4, :],
                                                silu_buf[:, j % 2], ALU.mult).then_inc(h_whole, 1)
                        if 0 < j < GROUPS - 1:
                            split_lo(dense_up(j + 1))
                        if j == 0:
                            split_lo(dense_up(1))
                        dve.wait_ge(h_hi_ready, j + 1)
                        rest_of(h_lo[:, j % 2], h_buf[:, j % 2], h_hi[:, j % 2]).then_inc(h_ready, 1)
                        split_lo(dense_down(j))
                    splits(MIX1_AT, MIX1_AT + 2)
                    layer_norm(1, MIX1_AT - 1)
                    transposed_rest(2, 2, 0)
                else:
                    layer_norm(2, at + 13)
                    transposed_rest(3, 0, 1)

            def bcast(a):
                return a.unsqueeze(2).to_broadcast([P, NT, E])

            dve.wait_ge(logits_done, 1)
            step(nc.vector.tensor_copy(logits, accp[:, 0, 0:NT * E].rearrange("p (n e) -> p n e", n=NT)))
            for values, peak, chosen in ((logits, top, first_oh), (rest, top2, second_oh)):
                if values is rest:
                    step(nc.vector.scalar_tensor_tensor(out=rest, in0=first_oh, scalar=-3.0e38, in1=logits,
                                                        op0=ALU.mult, op1=ALU.add))
                step(nc.vector.tensor_reduce(peak, values, X, ALU.max))
                step(nc.vector.tensor_tensor(tmp_e, values, bcast(peak), ALU.is_equal))
                step(nc.vector.tensor_tensor(tmp_e, tmp_e, rank[:], ALU.mult))
                step(nc.vector.tensor_reduce(best, tmp_e, X, ALU.max))
                step(nc.vector.tensor_tensor(chosen, tmp_e, bcast(best), ALU.is_equal))
            nc.vector.tensor_tensor(mask, first_oh, second_oh, ALU.add).then_inc(mask_ready, 1)
            nc.vector.tensor_tensor(gap, top2, top, ALU.subtract).then_inc(gap_ready, 1)
            dve.wait_ge(gap_exp, 1)
            step(nc.vector.tensor_scalar_add(den, exp_gap, 1.0))
            step(nc.vector.reciprocal(g_first, den))
            step(nc.vector.tensor_tensor(g_second, exp_gap, g_first, ALU.mult))
            nc.vector.tensor_tensor(combine, first_oh, bcast(g_first), ALU.mult)
            step(nc.vector.tensor_tensor(tmp_e, second_oh, bcast(g_second), ALU.mult))
            step(nc.vector.tensor_tensor(combine, combine, tmp_e, ALU.add))
            dve.wait_ge(pos_done, 1)
            nc.vector.tensor_copy(count_i[:], accp[0:1, 1, NT * E:(NT + 1) * E]).then_inc(counts_ready, 1)
            nc.vector.memset(slot_of[:, :, E:E + 1], -1000.0)
            step(nc.vector.scalar_tensor_tensor(out=slot_of[:, :, 0:E],
                                                in0=accp[:, 1, 0:NT * E].rearrange("p (n e) -> p n e", n=NT),
                                                scalar=1000.0, in1=mask, op0=ALU.add, op1=ALU.mult))
            step(nc.vector.tensor_scalar_add(slot_of[:, :, 0:E], slot_of[:, :, 0:E], -1000.0))
            choose(0)
            for n in range(NT):
                dve.wait_ge(x_hi_ready, n + 1)
                rest_of(x_lo[:, n, :], x[:, n, :], x_hi[:, n, :]).then_inc(x_lo_ready, 1)
                dve.wait_ge(x_lo_ready, n + 1)
                nc.vector.tensor_scalar(x[:, n, :], x[:, n, :], ALPHA, None, ALU.mult).then_inc(acc_added, 1)

            dve.wait_ge(counts_ready, 1)

            def expert(e, tiles):
                def split_e(first, last):
                    splits(MOE_AT + first, MOE_AT + last, e)

                def times_up(s):
                    dve.wait_ge(e_silu, e * STEPS + (s + 1))
                    used(MOE_AT + step_at(s) + 3, e)
                    if tiles == 1:
                        nc.vector.tensor_tensor(h_e[:, s % 2, :], turn[:, 2 * (s % 2) + 1, :], silu_e[:, s % 2, :],
                                                ALU.mult).then_inc(e_h, 1)
                    else:
                        nc.vector.tensor_tensor(h_e, turn[:, 1:4:2, :], silu_e, ALU.mult).then_inc(e_h, 1)

                def rest_of_h(s):
                    dve.wait_ge(e_hT_hi, e * STEPS + (s + 1))
                    if tiles == 1:
                        at = slice((s % 2) * BANK, (s % 2 + 1) * BANK)
                        rest_of(hT_lo[:, at], accp[:, 2 + s % 2, :], hT_hi[:, at]).then_inc(e_hT_lo, 1)
                    else:
                        lo, hi = (a[:, :].rearrange("p (o f) -> p o f", o=2) for a in (hT_lo, hT_hi))
                        rest_of(lo, turn[:, 0:4:2, :], hi).then_inc(e_hT_lo, 1)

                split_e(0, 0)
                dve.wait_ge(gathered, e * 2 + 2)
                nc.vector.tensor_copy(xg_lo[:, :, 0:tiles * P], (acc_half if tiles == 2 else turn[:, 2:4, :].rearrange(
                    "p b (k t) -> p (b k) t", t=P))).then_inc(xg_lo_ready, 1)
                split_e(1, 3)
                if tiles == 2:
                    times_up(0)
                    rest_of_h(0)
                for s in range(1, STEPS):
                    b = step_at(s)
                    if tiles == 1:
                        if s == 1:
                            split_e(b, b + 1)
                            times_up(0)
                            split_e(b + 2, b + 3)
                        else:
                            times_up(s - 1)
                            split_e(b, b + 3)
                        rest_of_h(s - 1)
                    else:
                        split_e(b, b + 3)
                    if s == 1:
                        choose(e + 1)
                    split_e(b + 4, b + 5)
                    if tiles == 2:
                        times_up(s)
                        rest_of_h(s)
                if tiles == 1:
                    times_up(STEPS - 1)
                split_e(E_PIECES - 2, E_PIECES - 1)
                if tiles == 1:
                    rest_of_h(STEPS - 1)
                dve.wait_ge(ys_hi_ready, e + 1)
                rest_of(ys_lo[:, 0:tiles, :], accp[:, 0:2 * tiles, :].rearrange("p (o b) c -> p o (b c)", o=tiles),
                        ys_hi[:, 0:tiles, :]).then_inc(ys_ready, 1)
                dve.wait_ge(acc_added, e * NT + NT)
                for n in range(NT):
                    dve.wait_ge(scattered, e * NT + n + 1)
                    nc.vector.scalar_tensor_tensor(out=x[:, n, :], in0=tile_sum(n), scalar=combine[:, n, ds(e, 1)],
                                                   in1=x[:, n, :], op0=ALU.mult, op1=ALU.add).then_inc(acc_added, 1)

            with dve.Fori(0, E) as e:
                many = dve.value_load(count_i[0:1, ds(e, 1)], min_val=0, max_val=TOK)
                with dve.If(many > P):
                    expert(e, 2)
                with dve.Else():
                    expert(e, 1)

            dve.wait_ge(acc_added, NT * (E + 1))
            dve.wait_ge(ln_reloaded, 32 * 3)
            for n in range(NT):
                statistics(x[:, n, :], n, 2 + n, D, LN_EPS, ln_var)
                dve.wait_ge(ln_rstd, NT * 3 + n + 1)
                step(nc.vector.tensor_scalar(x[:, n, :], x[:, n, :], mv[n][:, 0:1], rstd[:, 2 + n:3 + n],
                                             ALU.subtract, ALU.mult))
                step(nc.vector.tensor_tensor(x[:, n, :], x[:, n, :], ln_rows[:, 0, :], ALU.mult))
                nc.vector.tensor_tensor(x[:, n, :], x[:, n, :], ln_rows[:, 1, :], ALU.add).then_inc(out_ready, 1)

        @block.tensor
        def _(pe):
            def split(p, e=0):
                pe.wait_ge(split_done, upto(p, e))
                return w_hi[:, p % PARTS, :], w_lo[:, p % PARTS, :]

            def split_columns(p):
                return [a.rearrange("p (k f) -> p k f", k=KD) for a in split(p)]

            def split_rows(p, e=0):
                return [a.rearrange("p (j d) -> p j d", j=2) for a in split(p, e)]

            def product(to, left, right, start, stop, **group):
                (lh, ll), (rh, rl) = left, right
                nc.tensor.matmul(to, lh, rh, start=start, stop=False, **group)
                nc.tensor.matmul(to, lh, rl, start=False, stop=False, **group)
                return nc.tensor.matmul(to, ll, rh, start=False, stop=stop, **group)

            def transpose_x(build):
                for n in range(NT):
                    if build:
                        pe.wait_ge(ln_norm, NT * (build - 1) + n + 1)
                    for k in range(KD):
                        last = nc.tensor.transpose(turn[:, 2 * n + k // 4, (k % 4) * P:(k % 4 + 1) * P],
                                                   x[:, n, k * P:(k + 1) * P], ident[:])
                    last.then_inc(x_transposed, 1)

            def two_blocks(p, to):
                wh, wl = split_columns(p)
                for b in range(2):
                    at = slice(b * P, (b + 1) * P)
                    for k in range(KD):
                        last = product(to[:, b, :], (wh[:, k, at], wl[:, k, at]), (xT_hi[:, k, :], xT_lo[:, k, :]),
                                       k == 0, k == KD - 1)
                last.then_inc(piece_used, 1)

            def two_rows(p, left, first, last_one):
                wd = split_rows(p)
                for n in range(NT):
                    for half in range(2):
                        for j in range(2):
                            cols = slice(half * BANK, (half + 1) * BANK)
                            last = product(accp[:, 2 * n + half, :], [a[:, j, n * P:(n + 1) * P] for a in left],
                                           [a[:, j, cols] for a in wd], first and j == 0, last_one and j == 1)
                    if last_one and n == 0:
                        last.then_inc(sum_done, 1)
                last.then_inc(piece_used, 1)

            pe.wait_ge(ident_ready, 1)
            pe.wait_ge(x_loaded, 16)
            transpose_x(0)
            pe.wait_ge(chan_loaded, 16 * 6)
            nc.tensor.transpose(accp[:, 3, 0:N_CHAN], chan_rows[:], ident[0:N_CHAN, 0:N_CHAN]).then_inc(chan_transposed, 1)
            pe.wait_ge(ws_masked, 1)
            for i in range(DEPTH * HEADS):
                last = nc.tensor.transpose(accp[:, i // 4, (i % 4) * P:(i % 4 + 1) * P], ws_raw[:, i, :], ident[:])
            last.then_inc(ws_transposed, 1)
            pe.wait_ge(consts_ready, 1)
            pe.wait_ge(mean_conv_ready, 1)

            for l in range(DEPTH):
                at = l * MIX1_AT
                pe.wait_ge(xT_ready, NT * (2 * l + 1))
                for half in range(2):
                    wv = split_columns(at + half)
                    for n in range(NT):
                        for k in range(KD):
                            last = product(turn[:, n, half * HALF:(half + 1) * HALF],
                                           [a[:, k, n * P:(n + 1) * P] for a in (xT_hi, xT_lo)],
                                           [a[:, k, :] for a in wv], k == 0, k == KD - 1)
                    last.then_inc(piece_used, 1)
                for i in range(2):
                    two_blocks(at + 2 + i, turn_half[:, 4 + 2 * i:6 + 2 * i, :])
                pe.wait_ge(v_gelu, NT * (l + 1))
                for i in range(2):
                    two_blocks(at + 4 + i, turn_half[:, 2 * i:2 * i + 2, :])
                pe.wait_ge(v_ready, NT * (l + 1))
                if l == 0:
                    pe.wait_ge(wsT_ready, 1)
                for h in range(HEADS):
                    for n in range(NT):
                        last = nc.tensor.matmul(acc_half[:, h, n * P:(n + 1) * P], v[:, n, h * P:(h + 1) * P],
                                                wsT[:, l * HEADS + h, :], start=True, stop=True)
                last.then_inc(z_done, 1)
                pe.wait_ge(cg_ready, 2 * (l + 1))
                for i in range(2):
                    two_blocks(at + 6 + i, turn_half[:, 4 + 2 * i:6 + 2 * i, :])
                pe.wait_ge(q_ready, 2 * (l + 1))
                for i in range(2):
                    two_blocks(at + 8 + i, turn_half[:, 2 * i:2 * i + 2, :])
                    if i == 0:
                        for b in range(2):
                            pe.wait_ge(conv_squared, 2 * l + b + 1)
                            nc.tensor.matmul(turn[:, 2 + b, :], mean_conv[:], conv_sq[:, 2 * b:2 * b + 2, :].rearrange(
                                "p c t -> p (c t)"), start=True, stop=True).then_inc(conv_mean, 1)
                pe.wait_ge(zb_ready, l + 1)
                pe.wait_ge(y_ready, 2 * l + 1)
                for i in range(4):
                    if i == 1:
                        for b in range(2):
                            pe.wait_ge(gmlp_squared, 2 * l + b + 1)
                            nc.tensor.matmul(turn[:, b, :], mean_gmlp[:], gmlp_sq[:, 2 * b:2 * b + 2, :].rearrange(
                                "p c t -> p (c t)"), start=True, stop=True).then_inc(gmlp_mean, 1)
                    if i == 2:
                        pe.wait_ge(y_ready, 2 * l + 2)
                    two_rows(at + 10 + i, (y_hi[:, 2 * i:2 * i + 2, :], y_lo[:, 2 * i:2 * i + 2, :]), i == 0, i == 3)
                transpose_x(2 * l + 1)
                if l == 1:
                    break

                pe.wait_ge(xT_ready, 2 * NT)
                for j in range(GROUPS + 1):
                    if j < GROUPS:
                        for i, p in enumerate((dense_gate(j), dense_up(j))):
                            two_blocks(p, turn_half[:, 4 * (j % 2) + 2 * i:4 * (j % 2) + 2 * i + 2, :])
                    if j:
                        i = j - 1
                        pe.wait_ge(h_ready, i + 1)
                        two_rows(dense_down(i), (h_hi[:, i % 2], h_lo[:, i % 2]), i == 0, i == GROUPS - 1)
                transpose_x(2)

            pe.wait_ge(wr_loaded, 16)
            pe.wait_ge(xT_low, 3 * NT)
            pe.wait_ge(xT_high, 3 * NT)
            for n in range(NT):
                for k in range(KD):
                    last = nc.tensor.matmul(accp[:, 0, n * E:(n + 1) * E], xT[:, k, n * P:(n + 1) * P], wr[:, k, :],
                                            start=(k == 0), stop=(k == KD - 1))
            last.then_inc(logits_done, 1)
            pe.wait_ge(mask_ready, 1)
            nc.tensor.matmul(accp[:, 1, 0:E], before[:], mask[:, 0, :], start=True, stop=True)
            nc.tensor.matmul(accp[:, 1, E:2 * E], before[:], mask[:, 1, :], start=True, stop=False)
            nc.tensor.matmul(accp[:, 1, E:2 * E], ones[:], mask[:, 0, :], start=False, stop=True)
            nc.tensor.matmul(accp[:, 1, 2 * E:3 * E], ones[:], mask[:, 0, :], start=True, stop=False)
            nc.tensor.matmul(accp[:, 1, 2 * E:3 * E], ones[:], mask[:, 1, :], start=False, stop=True).then_inc(pos_done, 1)

            pe.wait_ge(counts_ready, 1)
            pe.wait_ge(x_lo_ready, NT)

            def expert(e, tiles):
                def gather(part, to):
                    for k in range(KD):
                        for n in range(NT):
                            last = nc.tensor.matmul(to[:, k, :], part[:, n, k * P:(k + 1) * P], pick[:, n, 0:tiles * P],
                                                    start=(n == 0), stop=(n == NT - 1))
                    last.then_inc(gathered, 1)

                def transpose_h(s):
                    pe.wait_ge(e_h, e * STEPS + (s + 1))
                    for o in range(tiles):
                        to = accp[:, 2 + s % 2, :] if tiles == 1 else turn[:, 2 * o, :]
                        src = h_e[:, s % 2 if tiles == 1 else o, :]
                        for b in range(COL // P):
                            last = nc.tensor.transpose(to[:, b * P:(b + 1) * P], src[:, b * P:(b + 1) * P], ident[:])
                    last.then_inc(e_hT, 1)

                def down(s):
                    pe.wait_ge(e_hT_lo, e * STEPS + (s + 1))
                    for half in range(2):
                        wd = split_rows(MOE_AT + step_down(s) + half, e)
                        for j in range(2):
                            b = 2 * half + j
                            for o in range(tiles):
                                at = (s % 2 if tiles == 1 else o) * BANK + b * P
                                for c in range(2):
                                    last = product(accp[:, 2 * o + c, :], [a[:, at:at + P] for a in (hT_hi, hT_lo)],
                                                   [a[:, j, c * BANK:(c + 1) * BANK] for a in wd],
                                                   s == 0 and b == 0, s == STEPS - 1 and b == 3)
                        last.then_inc(piece_used, 1)

                def half_step(s, which):
                    for half in range(2):
                        p = MOE_AT + step_at(s) + 2 * which + half
                        w = [a.rearrange("p (k f) -> p k f", k=KD // 2) for a in split(p, e)]
                        for o in range(tiles):
                            to = turn[:, 2 * (s % 2 if tiles == 1 else o) + which, :]
                            for kk in range(KD // 2):
                                k = half * (KD // 2) + kk
                                last = product(to, [a[:, k, o * P:(o + 1) * P] for a in (xg_hi, xg_lo)],
                                               [a[:, kk, :] for a in w], k == 0, k == KD - 1)
                        last.then_inc(piece_used, 1)

                pe.wait_ge(pick_ready, e + 1)
                if tiles == 1:
                    gather(x_hi, turn[:, 0:2, :].rearrange("p b (k t) -> p (b k) t", t=P))
                    gather(x_lo, turn[:, 2:4, :].rearrange("p b (k t) -> p (b k) t", t=P))
                    pe.wait_ge(acc_added, e * NT + NT)
                else:
                    gather(x_hi, turn_half)
                    pe.wait_ge(acc_added, e * NT + NT)
                    gather(x_lo, acc_half)
                    pe.wait_ge(xg_lo_ready, e + 1)
                for o in range(tiles):
                    for n in range(NT):
                        last = nc.tensor.transpose(accp[:, 2, o * TOK + n * P:o * TOK + (n + 1) * P],
                                                   pick[:, n, o * P:(o + 1) * P].bitcast(f32), ident[:])
                last.then_inc(pick_transposed, 1)
                pe.wait_ge(xg_hi_ready, e + 1)
                pe.wait_ge(xg_lo_ready, e + 1)
                pe.wait_ge(pickT_ready, e + 1)
                for s in range(STEPS):
                    half_step(s, 0)
                    if s and tiles == 1:
                        transpose_h(s - 1)
                    half_step(s, 1)
                    if s:
                        down(s - 1)
                    if tiles == 2:
                        transpose_h(s)
                        pe.wait_ge(e_hT_lo, e * STEPS + (s + 1))
                if tiles == 1:
                    transpose_h(STEPS - 1)
                down(STEPS - 1)
                pe.wait_ge(ys_ready, e + 1)
                for n in range(NT):
                    for half in range(2):
                        for o in range(tiles):
                            for i, part in enumerate((ys_hi, ys_lo)):
                                last = nc.tensor.matmul(accp[:, 2 * n + half, :], pickT[:, o, n * P:(n + 1) * P],
                                                        part[:, o, half * BANK:(half + 1) * BANK],
                                                        start=(o == 0 and i == 0), stop=(o == tiles - 1 and i == 1))
                    last.then_inc(scattered, 1)

            with pe.Fori(0, E) as e:
                many = pe.value_load(count_i[0:1, ds(e, 1)], min_val=0, max_val=TOK)
                with pe.If(many > P):
                    expert(e, 2)
                with pe.Else():
                    expert(e, 1)


_INS = ["x", "w_in", "conv_w", "v_g", "v_b", "w_s", "b_s", "out_g", "w_out", "ln1_g", "ln1_b", "ln2_g", "ln2_b",
        "w_gate", "w_up", "w_down", "w_router", "we_gate", "we_up", "we_down"]


def kernel(**inputs):
    import numpy as np
    import concourse.bacc as bacc
    from concourse.bass_utils import run_bass_kernel_spmd

    nc = bacc.Bacc("TRN2", target_bir_lowering=False, num_devices=1)
    arrays, args = {}, []
    for name in _INS:
        a = np.ascontiguousarray(inputs[name])
        arrays[f"in_{name}"] = a
        args.append(nc.dram_tensor(f"in_{name}", a.shape, mybir.dt.from_np(a.dtype), kind="ExternalInput").ap())
    shape = arrays["in_x"].shape
    out = nc.dram_tensor("out_x", shape, mybir.dt.float32, kind="ExternalOutput").ap()
    hybrid_trunk_kernel(nc, *args, out)
    r = run_bass_kernel_spmd(nc, [arrays], core_ids=[0])
    return r.results[0]["out_x"]
```

```python
import concourse.bass as bass
from concourse import mybir
from contextlib import ExitStack

P = 128
BANK = 512
DEPTH = 2
ALPHA = (2 * DEPTH) ** 0.25
LN_EPS = 1e-5
RMS_EPS = 1e-6
TOP_K = 2


def hybrid_trunk_kernel(nc, x_in, w_in, conv_w, v_g, v_b, w_s, b_s, out_g, w_out, ln1_g, ln1_b, ln2_g, ln2_b,
                        w_gate, w_up, w_down, w_router, we_gate, we_up, we_down, out):
    f32 = mybir.dt.float32
    f32r = mybir.dt.float32r
    i32 = mybir.dt.int32
    ALU = mybir.AluOpType
    ACT = mybir.ActivationFunctionType
    X = mybir.AxisListType.X
    ds = bass.ds

    _, TOK, D = x_in.shape
    NT = TOK // P
    KD = D // P
    CW = conv_w.shape[2]
    TAPS = conv_w.shape[1]
    CB = CW // P
    GW = v_g.shape[1]
    HEADS = w_s.shape[1]
    E = we_gate.shape[1]
    FF_D = w_gate.shape[2]
    FF_E = we_gate.shape[3]
    CONV_HD = 64

    PIECE = 2048
    RING = 7
    PARTS = 3
    HALF = 2 * P
    COL = 512
    MIX = 2 * 5 + 4
    GROUPS = FF_D // HALF
    STEPS = FF_E // COL
    E_PIECES = 6 * STEPS
    DENSE_AT = MIX
    MIX1_AT = DENSE_AT + 3 * GROUPS
    MOE_AT = MIX1_AT + MIX
    assert E_PIECES % RING == 0 and E_PIECES % PARTS == 0 and FF_D % HALF == 0 and FF_E % COL == 0
    TURNS = E_PIECES // RING

    def dense_gate(j):
        return DENSE_AT + (3 * j - 1 if j else 0)

    def dense_up(j):
        return dense_gate(j) + 1

    def dense_down(j):
        return dense_gate(j + 1) + 2 if j < GROUPS - 1 else MIX1_AT - 1

    def step_at(s):
        return 6 * s - 2 if s else 0

    def step_down(s):
        return step_at(s + 1) + 4 if s < STEPS - 1 else E_PIECES - 2

    ctx = ExitStack()
    with ctx:
        def sb(name, shape, dt=f32):
            return ctx.enter_context(nc.sbuf_tensor(name, shape, dt))

        def sem(name):
            return ctx.enter_context(nc.semaphore(name))

        raw = sb("raw", [P, RING, PIECE])
        w_hi = sb("w_hi", [P, PARTS, PIECE], f32r)
        w_lo = sb("w_lo", [P, PARTS, PIECE], f32r)
        x = sb("x", [P, NT, D])
        t_hi = sb("t_hi", [P, KD * TOK], f32r)
        t_lo = sb("t_lo", [P, KD * TOK], f32r)
        a_hi = sb("a_hi", [P, KD * TOK], f32r)
        a_lo = sb("a_lo", [P, KD * TOK], f32r)
        hT_hi = sb("hT_hi", [P, 4 * TOK], f32r)
        hT_lo = sb("hT_lo", [P, 4 * TOK], f32r)
        pick = sb("pick", [P, NT, TOK], f32r)
        pickT = sb("pickT", [P, NT, TOK], f32r)
        ln_rows = sb("ln_rows", [P, 2, D])
        v_rows = sb("v_rows", [P, 2, GW])
        bs_rows = sb("bs_rows", [P, DEPTH, HEADS, P])
        wsT = sb("wsT", [P, DEPTH * HEADS, P])
        work = sb("work", [P, 6160])
        ident = sb("ident", [P, P])
        mean_conv = sb("mean_conv", [P, P])
        mean_gmlp = sb("mean_gmlp", [P, P])
        before = sb("before", [P, P])
        ones = sb("ones", [P, P])
        N_CHAN = DEPTH * (TAPS * CB + 5 * KD)
        chan_rows = sb("chan_rows", [N_CHAN, P])
        chan = sb("chan", [P, N_CHAN])
        wr = sb("wr", [P, KD, E])
        slot_iota = sb("slot_iota", [P, TOK])
        rank = sb("rank", [P, NT, E])
        small = sb("small", [P, 208])
        eps_rms = sb("eps_rms", [P, 1])
        neg_half = sb("neg_half", [P, 1])
        count_i = sb("count_i", [1, E], i32)

        v = work[:, 0:1024].rearrange("p (n c) -> p n c", n=NT)
        gmlp_sq = work[:, 0:1024].rearrange("p (c t) -> p c t", c=CB)
        cg = work[:, 1024:2048].rearrange("p (c t) -> p c t", c=CB)
        conv = cg
        q = work[:, 2048:3080].rearrange("p (c t) -> p c t", c=CB)
        conv_sq = work[:, 2048:3072].rearrange("p (c t) -> p c t", c=CB)
        zb = work[:, 3088:4112].rearrange("p (h n t) -> p h n t", h=HEADS, n=NT)
        zb2 = work[:, 3088:4112].rearrange("p (c t) -> p c t", c=CB)
        y = work[:, 4112:6160].rearrange("p (c t) -> p c t", c=KD)
        ws_raw = work[:, 4112:5136].rearrange("p (l s) -> p l s", s=P)
        silu_buf = work[:, 4112:5136].rearrange("p (i c t) -> p i c t", i=2, c=2)
        h_buf = work[:, 5136:6160].rearrange("p (i c t) -> p i c t", i=2, c=2)
        silu_e = work[:, 4112:5136].rearrange("p (i f) -> p i f", i=2)
        h_e = work[:, 5136:6160].rearrange("p (i f) -> p i f", i=2)
        xT = work[:, 0:2048].rearrange("p (k t) -> p k t", k=KD)
        xT_hi, xT_lo, y_hi, y_lo, xg_hi, xg_lo = (
            a[:, :].rearrange("p (k t) -> p k t", k=KD) for a in (t_hi, t_lo, a_hi, a_lo, a_hi, a_lo))
        x_hi, x_lo, ys_hi, ys_lo = (
            a[:, :].rearrange("p (n d) -> p n d", n=NT) for a in (t_hi, t_lo, a_hi, a_lo))
        h_hi, h_lo = (a[:, 0:4 * TOK].rearrange("p (i b t) -> p i b t", i=2, b=2) for a in (a_hi, a_lo))
        stats = small[:, 0:12]
        mv = [small[:, 12:14], small[:, 14:16]]
        var_eps = small[:, 16:20]
        rstd = small[:, 20:24]
        shift = small[:, 24:26]
        logits = small[:, 32:48].rearrange("p (n e) -> p n e", n=NT)
        first_oh = small[:, 48:64].rearrange("p (n e) -> p n e", n=NT)
        second_oh = small[:, 64:80].rearrange("p (n e) -> p n e", n=NT)
        tmp_e = small[:, 80:96].rearrange("p (n e) -> p n e", n=NT)
        rest = small[:, 96:112].rearrange("p (n e) -> p n e", n=NT)
        combine = small[:, 112:128].rearrange("p (n e) -> p n e", n=NT)
        mask = small[:, 128:144].rearrange("p (n e) -> p n e", n=NT)
        slot_of = small[:, 144:162].rearrange("p (n e) -> p n e", n=NT)
        top = small[:, 164:166]
        top2 = small[:, 166:168]
        best = small[:, 168:170]
        gap = small[:, 170:172]
        exp_gap = small[:, 172:174]
        g_first = small[:, 174:176]
        g_second = small[:, 176:178]
        den = small[:, 178:180]

        O_G = DEPTH * TAPS * CB
        LN_C = [O_G + DEPTH * KD * (1 + i) for i in range(4)]

        def tap_col(l, k, c):
            i = (l * TAPS + k) * CB + c
            return chan[:, i:i + 1]

        def out_g_col(l, c):
            return chan[:, O_G + l * KD + c:O_G + l * KD + c + 1]

        def ln_col(which, l, k):
            i = LN_C[which] + l * KD + k
            return chan[:, i:i + 1]

        accp = ctx.enter_context(nc.psum_tensor("accp", [P, 4, BANK], f32))
        turn = ctx.enter_context(nc.psum_tensor("turn", [P, 4, BANK], f32))
        acc_half = accp[:, :, :].rearrange("p b (c s) -> p (b c) s", c=2)
        turn_half = turn[:, :, :].rearrange("p b (c s) -> p (b c) s", c=2)

        def tile_sum(n):
            return accp[:, 2 * n:2 * n + 2, :].rearrange("p b c -> p (b c)")

        slot_filled = [sem(f"slot_filled{i}") for i in range(RING)]
        low_affine = [sem(f"low_affine{n}") for n in range(NT)]
        high_affine = [sem(f"high_affine{n}") for n in range(NT)]
        x1_product, x1_affine = sem("x1_product"), sem("x1_affine")
        vrows_reloaded, ln_reloaded = sem("vrows_reloaded"), sem("ln_reloaded")
        hi_done, split_done, piece_used = sem("hi_done"), sem("split_done"), sem("piece_used")
        x_loaded = [sem(f"x_loaded{n}") for n in range(NT)]
        ws_loaded, chan_loaded, vrows_loaded, bs_loaded, ln_loaded, wr_loaded = (
            sem(n) for n in ("ws_loaded", "chan_loaded", "vrows_loaded", "bs_loaded", "ln_loaded",
                             "wr_loaded"))
        ident_zero, ident_ready, consts_ready, before_ones, ws_masked, mean_conv_ready = (
            sem(n) for n in ("ident_zero", "ident_ready", "consts_ready", "before_ones", "ws_masked",
                             "mean_conv_ready"))
        x_transposed, ws_transposed, chan_transposed = sem("x_transposed"), sem("ws_transposed"), sem("chan_transposed")
        wsT_ready, chan_ready, xT_hi_ready, xT_ready = (
            sem(n) for n in ("wsT_ready", "chan_ready", "xT_hi_ready", "xT_ready"))
        z_done, v_gelu, v_var, v_rstd, v_ready, cg_ready, q_ready, zb_ready, y_conv_raw = (
            sem(n) for n in ("z_done", "v_gelu", "v_var", "v_rstd", "v_ready", "cg_ready", "q_ready", "zb_ready",
                             "y_conv_raw"))
        u_gelu, y_gmlp_raw, conv_squared, gmlp_squared = (
            sem(n) for n in ("u_gelu", "y_gmlp_raw", "conv_squared", "gmlp_squared"))
        conv_mean, gmlp_mean, rms_log, rms_ready, y_normed, y_hi_ready, y_ready = (
            sem(n) for n in ("conv_mean", "gmlp_mean", "rms_log", "rms_ready", "y_normed", "y_hi_ready", "y_ready"))
        sum_done, ln_var, ln_rstd, ln_coef, ln_norm, x_affine, affine_step = (
            sem(n) for n in ("sum_done", "ln_var", "ln_rstd", "ln_coef", "ln_norm", "x_affine", "affine_step"))
        silu_ready, h_whole, h_hi_ready, h_ready = (sem(n) for n in ("silu_ready", "h_whole", "h_hi_ready", "h_ready"))
        logits_done, gap_ready, gap_exp, mask_ready, pos_done, counts_ready, pick_ready, x_hi_ready, x_lo_ready = (
            sem(n) for n in ("logits_done", "gap_ready", "gap_exp", "mask_ready", "pos_done", "counts_ready",
                             "pick_ready", "x_hi_ready", "x_lo_ready"))
        gathered, xg_hi_ready, xg_lo_ready, half_summed = (
            sem(n) for n in ("gathered", "xg_hi_ready", "xg_lo_ready", "half_summed"))
        slots_written, slots_read = sem("slots_written"), sem("slots_read")
        e_silu, e_h, e_hT, e_hT_hi, e_hT_lo, ys_hi_ready, ys_ready, scattered, acc_added = (
            sem(n) for n in ("e_silu", "e_h", "e_hT", "e_hT_hi", "e_hT_lo", "ys_hi_ready", "ys_ready", "scattered",
                             "acc_added"))
        out_scaled, out0_ready, out1_ready = sem("out_scaled"), sem("out0_ready"), sem("out1_ready")
        out_written, dve_step = sem("out_written"), sem("dve_step")

        def upto(p, e=0):
            return e * E_PIECES + (p + 1)

        def transposed(build, n, half=1):
            return 2 * (NT * build + n) + half + 1

        def added(e):
            return e * (2 * NT) + NT

        def out_half(tiles, half):
            if tiles == 2:
                return [a[:, :, half * BANK:(half + 1) * BANK] for a in (ys_hi, ys_lo)]
            at = (1 - half) * BANK
            return [a[:, at:at + BANK].unsqueeze(1) for a in (hT_hi, hT_lo)]

        def acc_half_tile(banks):
            return accp[:, banks:banks + 2, :].rearrange("p b (k t) -> p (b k) t", t=P)

        def first_slots(banks):
            return turn[:, banks:banks + 2, :].rearrange("p b (k t) -> p (b k) t", t=P)

        block = ctx.enter_context(nc.Block())

        @block.sync
        def _(sp):
            def load(p, src, e=0):
                if p >= RING:
                    sp.wait_ge(split_done, upto(p - RING, e))
                dst = raw[:, p % RING, :].rearrange("p (k f) -> p k f", k=src.shape[1])
                sp.dma_start(dst, src).then_inc(slot_filled[p % RING], 16)

            def columns(w, c0):
                return w[:, c0:c0 + HALF].rearrange("(k p) f -> p k f", p=P)

            def rows(w, r0):
                return w[r0:r0 + HALF, :].rearrange("(j p) d -> p j d", p=P)

            def mixer(at, l, between):
                for i, c0 in enumerate((3 * CW + GW, CW, 2 * CW, 0, 3 * CW)):
                    for half in range(2):
                        load(at + 2 * i + half, columns(w_in[l], c0 + half * HALF))
                    between(i)
                for i in range(4):
                    load(at + 10 + i, rows(w_out[l], i * HALF))

            def small_inputs(i):
                if i == 1:
                    sp.dma_start(ws_raw, w_s.rearrange("l h t s -> t (l h) s")).then_inc(ws_loaded, 16)
                if i == 0:
                    for j, a in enumerate((v_g, v_b)):
                        sp.dma_start(v_rows[:, j, :], a[0].partition_broadcast(P)).then_inc(vrows_loaded, 16)
                if i == 2:
                    sp.dma_start(bs_rows[:], b_s.partition_broadcast(P)).then_inc(bs_loaded, 16)
                if i == 4:
                    for j, a in enumerate((ln1_g, ln1_b)):
                        sp.dma_start(ln_rows[:, j, :], a[0].partition_broadcast(P)).then_inc(ln_loaded, 16)
                    sp.dma_start(wr[:], w_router[0].rearrange("(k p) e -> p k e", p=P)).then_inc(wr_loaded, 16)

            for n in range(NT):
                sp.dma_start(x[:, n, :], x_in[0, n * P:(n + 1) * P, :]).then_inc(x_loaded[n], 16)
            mixer(0, 0, small_inputs)
            for j in range(GROUPS):
                load(dense_gate(j), columns(w_gate[0], j * HALF))
                load(dense_up(j), columns(w_up[0], j * HALF))
                if j:
                    load(dense_down(j - 1), rows(w_down[0], (j - 1) * HALF))
            load(dense_down(GROUPS - 1), rows(w_down[0], (GROUPS - 1) * HALF))
            mixer(MIX1_AT, 1, lambda i: None)

            with sp.Fori(0, E) as e:
                wg, wu, wd = (w[0, ds(e, 1)].rearrange("o (k p) f -> p (o k) f", p=P) for w in (we_gate, we_up, we_down))
                for s in range(STEPS + 1):
                    if s < STEPS:
                        for i, w in enumerate((wg, wu)):
                            for half in range(2):
                                load(MOE_AT + step_at(s) + 2 * i + half,
                                     w[:, half * KD // 2:(half + 1) * KD // 2, s * COL:(s + 1) * COL], e)
                    if s:
                        for half in range(2):
                            j0 = 4 * (s - 1) + 2 * half
                            load(MOE_AT + step_down(s - 1) + half, wd[:, j0:j0 + 2, :], e)

            for n, half, ready, count in ((0, 1, out1_ready, 1), (0, 0, out0_ready, 1), (1, 0, out1_ready, 2),
                                          (1, 1, out1_ready, 3)):
                cols = slice(half * BANK, (half + 1) * BANK)
                sp.wait_ge(ready, count)
                sp.dma_start(out[0, n * P:(n + 1) * P, cols], x[:, n, cols]).then_inc(out_written, 16)
            sp.wait_ge(out_written, 16 * 2 * NT)

        @block.gpsimd
        def _(pool):
            nc.gpsimd.memset(ident[:], 0.0).then_inc(ident_zero, 1)
            pool.wait_ge(ident_zero, 1)
            nc.gpsimd.affine_select(out=ident[:], in_=ident[:], compare_op=ALU.not_equal, fill=1.0, base=0,
                                    pattern=[[-1, P]], channel_multiplier=1).then_inc(ident_ready, 1)
            nc.gpsimd.memset(neg_half[:], -0.5)
            nc.gpsimd.memset(eps_rms[:], RMS_EPS)
            nc.gpsimd.memset(mean_gmlp[:], 1.0 / P)
            nc.gpsimd.memset(before[:], 1.0)
            nc.gpsimd.memset(ones[:], 1.0)
            nc.gpsimd.iota(slot_iota[:], pattern=[[1, TOK]], base=0, channel_multiplier=0,
                           allow_small_or_imprecise_dtypes=True)
            nc.gpsimd.iota(rank[:], pattern=[[0, NT], [-1, E]], base=E, channel_multiplier=0,
                           allow_small_or_imprecise_dtypes=True).then_inc(before_ones, 1)
            pool.wait_ge(before_ones, 1)
            nc.gpsimd.affine_select(out=before[:], in_=before[:], compare_op=ALU.is_gt, fill=0.0, base=0,
                                    pattern=[[1, P]], channel_multiplier=-1).then_inc(consts_ready, 1)
            pool.wait_ge(ws_loaded, 16)
            nc.gpsimd.affine_select(out=ws_raw, in_=ws_raw, compare_op=ALU.is_ge, fill=0.0, base=0,
                                    pattern=[[0, DEPTH * HEADS], [-1, P]], channel_multiplier=1).then_inc(ws_masked, 1)

            def power(var_sem, rstd_sem, at, n):
                pool.wait_ge(var_sem, n)
                nc.gpsimd.tensor_tensor(rstd[:, at:at + 1], var_eps[:, at:at + 1], neg_half[:],
                                        ALU.pow).then_inc(rstd_sem, 1)

            def layer_norm(number, following):
                for n in range(NT):
                    power(ln_var, ln_rstd, 2 + n, NT * number + n + 1)
                pool.wait_ge(*((ln_reloaded, 32 * number) if number else (ln_loaded, 32)))
                for n in range(NT if number < 2 else 1):
                    pool.wait_ge(x_transposed, transposed(number + 1, n))
                    nc.gpsimd.tensor_tensor(x[:, n, :], x[:, n, :], ln_rows[:, 0, :],
                                            ALU.mult).then_inc(affine_step, 1)
                    pool.wait_ge(affine_step, NT * number + n + 1)
                    nc.gpsimd.tensor_tensor(x[:, n, :], x[:, n, :], ln_rows[:, 1, :], ALU.add).then_inc(x_affine, 1)
                pool.wait_ge(x_affine, NT * number + (NT if number < 2 else 1))
                if number == 2:
                    pool.wait_ge(x1_affine, 1)
                for i, a in enumerate(following):
                    pool.dma_start(ln_rows[:, i, :], a.partition_broadcast(P)).then_inc(ln_reloaded, 16)

            for l in range(DEPTH):
                for n in range(NT):
                    power(v_var, v_rstd, n, NT * l + n + 1)
                if l == 0:
                    pool.wait_ge(v_ready, NT)
                    for i, a in enumerate((v_g, v_b)):
                        pool.dma_start(v_rows[:, i, :], a[1].partition_broadcast(P)).then_inc(vrows_reloaded, 16)
                    layer_norm(0, (ln2_g[0], ln2_b[0]))
                    layer_norm(1, (ln1_g[1], ln1_b[1]))
                else:
                    layer_norm(2, (ln2_g[1], ln2_b[1]))
            for n in range(NT):
                pool.wait_ge(x_lo_ready, n + 1)
                nc.gpsimd.tensor_scalar(x[:, n, :], x[:, n, :], ALPHA, None, ALU.mult).then_inc(acc_added, 1)
            for n in range(NT):
                power(ln_var, ln_rstd, 2 + n, 3 * NT + n + 1)
            pool.wait_ge(out_scaled, 1)
            pool.wait_ge(ln_rstd, 3 * NT + 1)
            pool.wait_ge(ln_reloaded, 32 * 3)
            nc.gpsimd.tensor_scalar(x[:, 0, 0:BANK], x[:, 0, 0:BANK], rstd[:, 2:3], None,
                                    ALU.mult).then_inc(out_scaled, 1)
            pool.wait_ge(out_scaled, 2)
            nc.gpsimd.tensor_tensor(x[:, 0, 0:BANK], x[:, 0, 0:BANK], ln_rows[:, 1, 0:BANK],
                                    ALU.add).then_inc(out0_ready, 1)

        @block.scalar
        def _(act):
            r0 = 0
            for src in (conv_w.rearrange("l k (c p) -> (l k c) p", p=P),
                        *(a.rearrange("l (c p) -> (l c) p", p=P) for a in (out_g, ln1_g, ln1_b, ln2_g, ln2_b))):
                n = src.shape[0]
                act.dma_start(chan_rows[r0:r0 + n, :], src).then_inc(chan_loaded, 16)
                r0 += n

            def split_hi(p, e=0):
                act.wait_ge(slot_filled[p % RING], e * (16 * TURNS) + 16 * (p // RING + 1))
                if p >= PARTS:
                    act.wait_ge(piece_used, upto(p - PARTS, e))
                nc.scalar.copy(w_hi[:, p % PARTS, :], raw[:, p % RING, :]).then_inc(hi_done, 1)

            def splits(first, last, e=0):
                for p in range(first, last + 1):
                    split_hi(p, e)

            def used(p, e=0):
                act.wait_ge(piece_used, upto(p, e))

            def round_xT(build, n, half, source):
                nc.scalar.copy(xT_hi[:, 4 * half:4 * half + 4, n * P:(n + 1) * P], source).then_inc(xT_hi_ready, 1)

            def normalise_transposed(build, which, l, early=None):
                for n in range(NT):
                    act.wait_ge(ln_coef, NT * (build - 1) + n + 1)
                    for half in range(2):
                        cols = slice(half * D // 2, (half + 1) * D // 2)
                        nc.scalar.activation(x[:, n, cols], x[:, n, cols], ACT.Identity, bias=shift[:, n:n + 1],
                                             scale=rstd[:, 2 + n:3 + n]).then_inc(ln_norm, 1)
                    if n and early is not None:
                        split_hi(early)
                    at = slice(n * P, (n + 1) * P)
                    for half in range(2 - n):
                        act.wait_ge(x_transposed, transposed(build, n, half))
                        for k in range(4):
                            i = 4 * half + k
                            last = nc.scalar.activation(xT[:, i, at], turn[:, 2 * n + half, k * P:(k + 1) * P],
                                                        ACT.Identity, bias=ln_col(which + 1, l, i),
                                                        scale=ln_col(which, l, i))
                        last.then_inc((high_affine if half else low_affine)[n], 1)
                    if build < 3:
                        act.wait_ge(low_affine[n], build)
                        round_xT(build, n, 0, xT[:, 0:4, at])
                        act.wait_ge(high_affine[n], build)
                        round_xT(build, n, 1, xT[:, 4:8, at])

            for n in range(NT):
                for half in range(2):
                    act.wait_ge(x_transposed, transposed(0, n, half))
                    round_xT(0, n, half, turn[:, 2 * n + half, :].rearrange("p (k t) -> p k t", t=P))
            splits(0, 2)
            for l in range(DEPTH):
                at = l * MIX1_AT
                for n in range(NT):
                    used(at + n)
                    nc.scalar.activation(v[:, n, :], accp[:, n, :], ACT.Gelu).then_inc(v_gelu, 1)
                    split_hi(at + 3 + n)
                for i in range(2):
                    used(at + 2 + i)
                    nc.scalar.copy(cg[:, 2 * i:2 * i + 2, :],
                                   turn_half[:, 4 + 2 * i:6 + 2 * i, :]).then_inc(cg_ready, 1)
                    split_hi(at + 5 + i)
                split_hi(at + 7)
                splits(at + 8, at + 9)
                for i in range(2):
                    act.wait_ge(y_conv_raw, 2 * l + i + 1)
                    nc.scalar.activation(conv_sq[:, 2 * i:2 * i + 2, :], y[:, 2 * i:2 * i + 2, :],
                                         ACT.Square).then_inc(conv_squared, 1)
                splits(at + 10, at + 11)

                def roots(group, mean_sem, means, buf):
                    for i in range(2):
                        act.wait_ge(mean_sem, 2 * l + i + 1)
                        nc.scalar.activation(buf[:, 2 * i:2 * i + 2, :], means[:, 2 * i:2 * i + 2, :],
                                             ACT.Ln, bias=eps_rms[:]).then_inc(rms_log, 1)
                    for i in range(2):
                        act.wait_ge(rms_log, 4 * l + 2 * group + i + 1)
                        nc.scalar.activation(buf[:, 2 * i:2 * i + 2, :], buf[:, 2 * i:2 * i + 2, :], ACT.Exp,
                                             scale=-0.5).then_inc(rms_ready, 1)

                def round_y(group, i):
                    act.wait_ge(y_normed, 4 * l + 2 * group + i + 1)
                    c = CB * group + 2 * i
                    nc.scalar.copy(y_hi[:, c:c + 2, :], y[:, c:c + 2, :]).then_inc(y_hi_ready, 1)

                if l == 0:
                    act.wait_ge(consts_ready, 1)
                roots(0, conv_mean, acc_half[:, 0:4, :], conv)
                round_y(0, 0)
                round_y(0, 1)
                for i in range(2):
                    used(at + 8 + i)
                    nc.scalar.activation(y[:, CB + 2 * i:CB + 2 * i + 2, :], turn_half[:, 2 * i:2 * i + 2, :],
                                         ACT.Gelu).then_inc(u_gelu, 1)
                for i in range(2):
                    act.wait_ge(y_gmlp_raw, 2 * l + i + 1)
                    nc.scalar.activation(gmlp_sq[:, 2 * i:2 * i + 2, :], y[:, CB + 2 * i:CB + 2 * i + 2, :],
                                         ACT.Square).then_inc(gmlp_squared, 1)
                split_hi(at + 12)
                roots(1, gmlp_mean, turn_half[:, 4:8, :], zb2)
                round_y(1, 0)
                split_hi(at + 13)
                round_y(1, 1)
                split_hi(at + 14)
                if l == 0:
                    act.wait_ge(chan_ready, 1)
                    normalise_transposed(1, 0, 0)
                    splits(at + 15, at + 16)
                    for j in range(GROUPS):
                        if 0 < j < GROUPS - 1:
                            split_hi(dense_gate(j + 1))
                        if j == GROUPS - 1:
                            split_hi(dense_down(j))
                        used(dense_up(j))
                        nc.scalar.activation(silu_buf[:, j % 2], turn_half[:, 4 * (j % 2):4 * (j % 2) + 2, :],
                                             ACT.Silu).then_inc(silu_ready, 1)
                        if 0 < j < GROUPS - 1:
                            split_hi(dense_up(j + 1))
                        if j == 0:
                            split_hi(dense_up(1))
                        act.wait_ge(h_whole, j + 1)
                        nc.scalar.copy(h_hi[:, j % 2], h_buf[:, j % 2]).then_inc(h_hi_ready, 1)
                        if j < GROUPS - 1:
                            split_hi(dense_down(j))
                    split_hi(MIX1_AT)
                    normalise_transposed(2, 2, 0, early=MIX1_AT + 1)
                    split_hi(MIX1_AT + 2)
                else:
                    normalise_transposed(3, 0, 1)
                    split_hi(MOE_AT + 1)

            for n in range(NT):
                act.wait_ge(x1_affine if n else x_affine, 1 if n else NT * 2 + 1)
                nc.scalar.copy(x_hi[:, n, :], x[:, n, :]).then_inc(x_hi_ready, 1)
            split_hi(MOE_AT + 2)
            act.wait_ge(gap_ready, 1)
            nc.scalar.activation(exp_gap, gap, ACT.Exp).then_inc(gap_exp, 1)

            act.wait_ge(counts_ready, 1)

            def expert(e, tiles):
                def split_e(first, last):
                    splits(MOE_AT + first, MOE_AT + last, e)

                def silu_step(s):
                    used(MOE_AT + step_at(s) + 1, e)
                    for o in range(tiles):
                        i = s % 2 if tiles == 1 else o
                        last = nc.scalar.activation(silu_e[:, i, :], turn[:, 2 * i, :], ACT.Silu)
                    last.then_inc(e_silu, 1)

                def round_h(s):
                    act.wait_ge(e_hT, e * STEPS + (s + 1))
                    if tiles == 1:
                        nc.scalar.copy(hT_hi[:, (s % 2) * BANK:(s % 2 + 1) * BANK],
                                       accp[:, 2 + s % 2, :]).then_inc(e_hT_hi, 1)
                    else:
                        nc.scalar.copy(hT_hi[:, :].rearrange("p (o f) -> p o f", o=2),
                                       turn[:, 0:4:2, :]).then_inc(e_hT_hi, 1)

                if tiles == 2:
                    act.wait_ge(slots_written, e * 2 + 1)
                    nc.scalar.copy(xg_hi[:, :, P:], acc_half_tile(0))
                    nc.scalar.copy(xg_lo[:, :, P:], acc_half_tile(2)).then_inc(slots_read, 1)
                    act.wait_ge(slots_written, e * 2 + 2)
                    nc.scalar.copy(pickT[:], accp[:, 2, :].rearrange("p (o t) -> p o t", o=2)).then_inc(slots_read, 1)
                split_e(3, 3)
                if tiles == 1:
                    for n in range(NT):
                        act.wait_ge(slots_written, e * 2 + n + 1)
                        nc.scalar.copy(pickT[:, 0, n * P:(n + 1) * P],
                                       accp[:, 2 + n, 0:P]).then_inc(slots_read, 1)
                silu_step(0)
                if tiles == 2:
                    round_h(0)
                for s in range(1, STEPS):
                    b = step_at(s)
                    split_e(b, b + 3)
                    silu_step(s)
                    if tiles == 1:
                        round_h(s - 1)
                    split_e(b + 4, b + 5)
                    if tiles == 2:
                        round_h(s)
                split_e(E_PIECES - 2, E_PIECES - 2)
                if tiles == 1:
                    round_h(STEPS - 1)
                split_e(E_PIECES - 1, E_PIECES - 1)
                with act.If(e < E - 1):
                    split_e(E_PIECES, E_PIECES + 1)
                for half in range(2):
                    if half == 0:
                        act.wait_ge(half_summed, e + 1)
                    else:
                        used(MOE_AT + E_PIECES - 1, e)
                    hi, _ = out_half(tiles, half)
                    for o in range(tiles):
                        last = nc.scalar.copy(hi[:, o, :], accp[:, 2 * o + half, :])
                    last.then_inc(ys_hi_ready, 1)
                with act.If(e < E - 1):
                    if tiles == 2:
                        act.wait_ge(scattered, e * 2 + 2)
                    first_tokens(e + 1)
                    split_e(E_PIECES + 2, E_PIECES + 2)

            def first_tokens(e):
                act.wait_ge(gathered, e * 2 + 1)
                nc.scalar.copy(xg_hi[:, :, 0:P], first_slots(0)).then_inc(xg_hi_ready, 1)

            first_tokens(0)
            with act.Fori(0, E) as e:
                many = act.value_load(count_i[0:1, ds(e, 1)], min_val=0, max_val=TOK)
                with act.If(many > P):
                    expert(e, 2)
                with act.Else():
                    expert(e, 1)

        @block.vector
        def _(dve):
            steps = [0]

            def step(ins):
                steps[0] += 1
                ins.then_inc(dve_step, 1)
                dve.wait_ge(dve_step, steps[0])

            def rest_of(out, whole, hi):
                return nc.vector.tensor_tensor(out, whole, hi.bitcast(f32), ALU.subtract)

            def split_lo(p, e=0):
                dve.wait_ge(hi_done, upto(p, e))
                rest_of(w_lo[:, p % PARTS, :], raw[:, p % RING, :], w_hi[:, p % PARTS, :]).then_inc(split_done, 1)

            def splits(first, last, e=0):
                for p in range(first, last + 1):
                    split_lo(p, e)

            def used(p, e=0):
                dve.wait_ge(piece_used, upto(p, e))

            def rest_of_xT(build, n, half, source):
                dve.wait_ge(xT_hi_ready, transposed(build, n, half))
                at = slice(n * P, (n + 1) * P)
                rest_of(xT_lo[:, 4 * half:4 * half + 4, at], source,
                        xT_hi[:, 4 * half:4 * half + 4, at]).then_inc(xT_ready, 1)

            def statistics(rows_ap, n, at, width, eps, var_sem):
                for i in range(width // 512):
                    last = nc.vector.bn_stats(stats[:, 6 * i:6 * i + 6], rows_ap[:, i * 512:(i + 1) * 512])
                step(last)
                variance(n, at, width // 512, eps, var_sem)

            def variance(n, at, parts, eps, var_sem):
                step(nc.vector.bn_aggr(mv[n], stats[:, 0:6 * parts]))
                nc.vector.tensor_scalar_add(var_eps[:, at:at + 1], mv[n][:, 1:2], eps).then_inc(var_sem, 1)

            def coefficients(number, n):
                dve.wait_ge(ln_rstd, NT * number + n + 1)
                nc.vector.scalar_tensor_tensor(out=shift[:, n:n + 1], in0=mv[n][:, 0:1], scalar=-1.0,
                                               in1=rstd[:, 2 + n:3 + n], op0=ALU.mult, op1=ALU.mult).then_inc(ln_coef, 1)

            def layer_norm(number, last_piece, which, l, first, second=None):
                build = number + 1
                for n in range(NT):
                    if number:
                        dve.wait_ge(x_affine, NT * (number - 1) + n + 1)
                    for half in range(2):
                        if n and half:
                            used(last_piece)
                        else:
                            dve.wait_ge(sum_done, 3 * number + 2 * n + half + 1)
                        cols = slice(half * BANK, (half + 1) * BANK)
                        step(nc.vector.scalar_tensor_tensor(out=x[:, n, cols], in0=x[:, n, cols], scalar=ALPHA,
                                                            in1=accp[:, 2 * n + half, :], op0=ALU.mult, op1=ALU.add))
                        last = nc.vector.bn_stats(stats[:, 6 * half:6 * half + 6], x[:, n, cols])
                    step(last)
                    variance(n, 2 + n, 2, LN_EPS, ln_var)
                    if n == 0:
                        coefficients(number, 0)
                        if second is not None:
                            split_lo(first)
                if build < 3:
                    rest_of_xT(build, 0, 0, xT[:, 0:4, 0:P])
                coefficients(number, 1)
                if build < 3:
                    rest_of_xT(build, 0, 1, xT[:, 4:8, 0:P])
                split_lo(first if second is None else second)
                dve.wait_ge(x_transposed, transposed(build, 1, 1))
                for k in range(4):
                    last = nc.vector.tensor_scalar(xT[:, 4 + k, P:TOK], turn[:, 3, k * P:(k + 1) * P],
                                                   ln_col(which, l, 4 + k), ln_col(which + 1, l, 4 + k),
                                                   ALU.mult, ALU.add)
                last.then_inc(high_affine[1], 1)
                if build < 3:
                    for half in range(2):
                        rest_of_xT(build, 1, half, xT[:, 4 * half:4 * half + 4, P:TOK])

            def choose(e):
                for n in range(NT):
                    last = nc.vector.tensor_scalar(pick[:, n, :], slot_iota[:], slot_of[:, n, ds(e, 1)], None,
                                                   ALU.is_equal)
                last.then_inc(pick_ready, 1)

            step(nc.vector.memset(mean_conv[:], 0.0))
            for h in range(P // CONV_HD):
                a = h * CONV_HD
                last = nc.vector.memset(mean_conv[a:a + CONV_HD, a:a + CONV_HD], 1.0 / CONV_HD)
            last.then_inc(mean_conv_ready, 1)
            for n in range(NT):
                for half in range(2):
                    rest_of_xT(0, n, half, turn[:, 2 * n + half, :].rearrange("p (k t) -> p k t", t=P))
            splits(0, 2)

            for l in range(DEPTH):
                at = l * MIX1_AT
                nc.vector.memset(q[:, :, 0:TAPS - 1], 0.0)
                dve.wait_ge(vrows_reloaded if l else vrows_loaded, 32)
                for n in range(NT):
                    dve.wait_ge(v_gelu, NT * l + n + 1)
                    statistics(v[:, n, :], n, n, GW, LN_EPS, v_var)
                    dve.wait_ge(v_rstd, NT * l + n + 1)
                    step(nc.vector.tensor_scalar(v[:, n, :], v[:, n, :], mv[n][:, 0:1], rstd[:, n:n + 1],
                                                 ALU.subtract, ALU.mult))
                    step(nc.vector.tensor_tensor(v[:, n, :], v[:, n, :], v_rows[:, 0, :], ALU.mult))
                    nc.vector.tensor_tensor(v[:, n, :], v[:, n, :], v_rows[:, 1, :], ALU.add).then_inc(v_ready, 1)
                    split_lo(at + 3 + n)
                if l == 0:
                    dve.wait_ge(chan_transposed, 1)
                    nc.vector.tensor_copy(chan[:], accp[:, 1, 0:N_CHAN]).then_inc(chan_ready, 1)
                    dve.wait_ge(ws_transposed, 1)
                    nc.vector.tensor_copy(wsT[:], accp[:, 2:4, :].rearrange("p b (l s) -> p (b l) s",
                                                                           s=P)).then_inc(wsT_ready, 1)
                for i in range(2):
                    split_lo(at + 5 + i)
                    dve.wait_ge(cg_ready, 2 * l + i + 1)
                    used(at + 4 + i)
                    nc.vector.tensor_tensor(q[:, 2 * i:2 * i + 2, 2:], turn_half[:, 2 * i:2 * i + 2, :],
                                            cg[:, 2 * i:2 * i + 2, :], ALU.mult).then_inc(q_ready, 1)
                split_lo(at + 7)
                dve.wait_ge(q_ready, 2 * l + 2)
                if l == 0:
                    dve.wait_ge(chan_ready, 1)
                for c in range(CB):
                    last = nc.vector.tensor_scalar(conv[:, c, :], q[:, c, 0:TOK], tap_col(l, 0, c), None, ALU.mult)
                step(last)
                for k in range(1, TAPS):
                    for c in range(CB):
                        last = nc.vector.scalar_tensor_tensor(out=conv[:, c, :], in0=q[:, c, k:k + TOK],
                                                              scalar=tap_col(l, k, c), in1=conv[:, c, :],
                                                              op0=ALU.mult, op1=ALU.add)
                    step(last)
                split_lo(at + 8)
                for i in range(2):
                    used(at + 6 + i)
                    nc.vector.tensor_tensor(y[:, 2 * i:2 * i + 2, :], turn_half[:, 4 + 2 * i:6 + 2 * i, :],
                                            conv[:, 2 * i:2 * i + 2, :], ALU.mult).then_inc(y_conv_raw, 1)
                splits(at + 9, at + 11)

                def over_rms(group, buf):
                    c0 = CB * group
                    for i in range(2):
                        dve.wait_ge(rms_ready, 4 * l + 2 * group + i + 1)
                        for c in (2 * i, 2 * i + 1):
                            last = nc.vector.scalar_tensor_tensor(out=y[:, c0 + c, :], in0=y[:, c0 + c, :],
                                                                  scalar=out_g_col(l, c0 + c), in1=buf[:, c, :],
                                                                  op0=ALU.mult, op1=ALU.mult)
                        last.then_inc(y_normed, 1)

                def rest_of_y(group, i):
                    dve.wait_ge(y_hi_ready, 4 * l + 2 * group + i + 1)
                    c = CB * group + 2 * i
                    rest_of(y_lo[:, c:c + 2, :], y[:, c:c + 2, :], y_hi[:, c:c + 2, :]).then_inc(y_ready, 1)

                dve.wait_ge(bs_loaded, 16)
                dve.wait_ge(z_done, l + 1)
                for i in range(2):
                    for n in range(NT):
                        last = nc.vector.tensor_tensor(zb[:, 2 * i:2 * i + 2, n, :],
                                                       acc_half[:, CB + 2 * i:CB + 2 * i + 2, n * P:(n + 1) * P],
                                                       bs_rows[:, l, 2 * i:2 * i + 2, :], ALU.add)
                last.then_inc(zb_ready, 1)
                dve.wait_ge(y_conv_raw, 2 * l + 2)
                over_rms(0, conv)
                rest_of_y(0, 0)
                rest_of_y(0, 1)
                dve.wait_ge(zb_ready, l + 1)
                for i in range(2):
                    dve.wait_ge(u_gelu, 2 * l + i + 1)
                    nc.vector.tensor_tensor(y[:, CB + 2 * i:CB + 2 * i + 2, :], y[:, CB + 2 * i:CB + 2 * i + 2, :],
                                            zb2[:, 2 * i:2 * i + 2, :], ALU.mult).then_inc(y_gmlp_raw, 1)
                split_lo(at + 12)
                dve.wait_ge(y_gmlp_raw, 2 * l + 2)
                over_rms(1, zb2)
                rest_of_y(1, 0)
                split_lo(at + 13)
                rest_of_y(1, 1)
                if l == 0:
                    layer_norm(0, at + 13, 0, 0, at + 14)
                    splits(at + 15, at + 16)
                    for j in range(GROUPS):
                        if 0 < j < GROUPS - 1:
                            split_lo(dense_gate(j + 1))
                        if j == GROUPS - 1:
                            split_lo(dense_down(j))
                        dve.wait_ge(silu_ready, j + 1)
                        nc.vector.tensor_tensor(h_buf[:, j % 2], turn_half[:, 4 * (j % 2) + 2:4 * (j % 2) + 4, :],
                                                silu_buf[:, j % 2], ALU.mult).then_inc(h_whole, 1)
                        if 0 < j < GROUPS - 1:
                            split_lo(dense_up(j + 1))
                        if j == 0:
                            split_lo(dense_up(1))
                        dve.wait_ge(h_hi_ready, j + 1)
                        rest_of(h_lo[:, j % 2], h_buf[:, j % 2], h_hi[:, j % 2]).then_inc(h_ready, 1)
                        if j < GROUPS - 1:
                            split_lo(dense_down(j))
                    layer_norm(1, MIX1_AT - 1, 2, 0, MIX1_AT, MIX1_AT + 1)
                    split_lo(MIX1_AT + 2)
                else:
                    layer_norm(2, at + 13, 0, 1, MOE_AT)
                    dve.wait_ge(ln_reloaded, 32 * 2)
                    nc.vector.tensor_tensor(x[:, 1, :], x[:, 1, :], ln_rows[:, 0, :], ALU.mult).then_inc(x1_product, 1)
                    dve.wait_ge(x1_product, 1)
                    nc.vector.tensor_tensor(x[:, 1, :], x[:, 1, :], ln_rows[:, 1, :], ALU.add).then_inc(x1_affine, 1)

            def bcast(a):
                return a.unsqueeze(2).to_broadcast([P, NT, E])

            dve.wait_ge(logits_done, 1)
            step(nc.vector.tensor_copy(logits, accp[:, 0, 0:NT * E].rearrange("p (n e) -> p n e", n=NT)))
            for values, peak, chosen in ((logits, top, first_oh), (rest, top2, second_oh)):
                if values is rest:
                    step(nc.vector.scalar_tensor_tensor(out=rest, in0=first_oh, scalar=-3.0e38, in1=logits,
                                                        op0=ALU.mult, op1=ALU.add))
                step(nc.vector.tensor_reduce(peak, values, X, ALU.max))
                step(nc.vector.tensor_tensor(tmp_e, values, bcast(peak), ALU.is_equal))
                step(nc.vector.tensor_tensor(tmp_e, tmp_e, rank[:], ALU.mult))
                step(nc.vector.tensor_reduce(best, tmp_e, X, ALU.max))
                step(nc.vector.tensor_tensor(chosen, tmp_e, bcast(best), ALU.is_equal))
            nc.vector.tensor_tensor(mask, first_oh, second_oh, ALU.add).then_inc(mask_ready, 1)
            nc.vector.tensor_tensor(gap, top2, top, ALU.subtract).then_inc(gap_ready, 1)
            for n in range(NT):
                dve.wait_ge(x_hi_ready, n + 1)
                rest_of(x_lo[:, n, :], x[:, n, :], x_hi[:, n, :]).then_inc(x_lo_ready, 1)
            dve.wait_ge(pos_done, 1)
            nc.vector.tensor_copy(count_i[:], accp[0:1, 1, NT * E:(NT + 1) * E]).then_inc(counts_ready, 1)
            nc.vector.memset(slot_of[:, :, E:E + 1], -1000.0)
            step(nc.vector.scalar_tensor_tensor(out=slot_of[:, :, 0:E],
                                                in0=accp[:, 1, 0:NT * E].rearrange("p (n e) -> p n e", n=NT),
                                                scalar=1000.0, in1=mask, op0=ALU.add, op1=ALU.mult))
            step(nc.vector.tensor_scalar_add(slot_of[:, :, 0:E], slot_of[:, :, 0:E], -1000.0))
            choose(0)
            split_lo(MOE_AT + 1)
            dve.wait_ge(counts_ready, 1)

            def expert(e, tiles):
                def split_e(first, last):
                    splits(MOE_AT + first, MOE_AT + last, e)

                def times_up(s):
                    dve.wait_ge(e_silu, e * STEPS + (s + 1))
                    used(MOE_AT + step_at(s) + 3, e)
                    if tiles == 1:
                        nc.vector.tensor_tensor(h_e[:, s % 2, :], turn[:, 2 * (s % 2) + 1, :], silu_e[:, s % 2, :],
                                                ALU.mult).then_inc(e_h, 1)
                    else:
                        nc.vector.tensor_tensor(h_e, turn[:, 1:4:2, :], silu_e, ALU.mult).then_inc(e_h, 1)

                def rest_of_h(s):
                    dve.wait_ge(e_hT_hi, e * STEPS + (s + 1))
                    if tiles == 1:
                        at = slice((s % 2) * BANK, (s % 2 + 1) * BANK)
                        rest_of(hT_lo[:, at], accp[:, 2 + s % 2, :], hT_hi[:, at]).then_inc(e_hT_lo, 1)
                    else:
                        lo, hi = (a[:, :].rearrange("p (o f) -> p o f", o=2) for a in (hT_lo, hT_hi))
                        rest_of(lo, turn[:, 0:4:2, :], hi).then_inc(e_hT_lo, 1)

                split_e(3, 3)
                if tiles == 2:
                    times_up(0)
                    rest_of_h(0)
                for s in range(1, STEPS):
                    b = step_at(s)
                    if tiles == 1:
                        if s == 1:
                            split_e(b, b + 1)
                            times_up(0)
                            split_e(b + 2, b + 3)
                        else:
                            times_up(s - 1)
                            split_e(b, b + 3)
                        rest_of_h(s - 1)
                    else:
                        split_e(b, b + 3)
                    if s == 1:
                        choose(e + 1)
                    split_e(b + 4, b + 5)
                    if tiles == 2:
                        times_up(s)
                        rest_of_h(s)
                if tiles == 1:
                    times_up(STEPS - 1)
                split_e(E_PIECES - 2, E_PIECES - 2)
                if tiles == 1:
                    rest_of_h(STEPS - 1)
                split_e(E_PIECES - 1, E_PIECES - 1)
                with dve.If(e < E - 1):
                    split_e(E_PIECES, E_PIECES + 1)
                for half in range(2):
                    dve.wait_ge(ys_hi_ready, e * 2 + half + 1)
                    hi, lo = out_half(tiles, half)
                    for o in range(tiles):
                        last = rest_of(lo[:, o, :], accp[:, 2 * o + half, :], hi[:, o, :])
                    last.then_inc(ys_ready, 1)
                with dve.If(e < E - 1):
                    if tiles == 2:
                        dve.wait_ge(scattered, e * 2 + 2)
                    first_tokens(e + 1)
                    split_e(E_PIECES + 2, E_PIECES + 2)

            def first_tokens(e):
                dve.wait_ge(gathered, e * 2 + 2)
                nc.vector.tensor_copy(xg_lo[:, :, 0:P], first_slots(2)).then_inc(xg_lo_ready, 1)

            first_tokens(0)
            split_lo(MOE_AT + 2)
            dve.wait_ge(gap_exp, 1)
            step(nc.vector.tensor_scalar_add(den, exp_gap, 1.0))
            step(nc.vector.reciprocal(g_first, den))
            step(nc.vector.tensor_tensor(g_second, exp_gap, g_first, ALU.mult))
            nc.vector.tensor_tensor(combine, first_oh, bcast(g_first), ALU.mult)
            step(nc.vector.tensor_tensor(tmp_e, second_oh, bcast(g_second), ALU.mult))
            step(nc.vector.tensor_tensor(combine, combine, tmp_e, ALU.add))

            with dve.Fori(0, E) as e:
                many = dve.value_load(count_i[0:1, ds(e, 1)], min_val=0, max_val=TOK)
                with dve.If(many > P):
                    expert(e, 2)
                with dve.Else():
                    expert(e, 1)
                dve.wait_ge(acc_added, added(e))
                for half in range(2):
                    dve.wait_ge(scattered, e * 2 + half + 1)
                    cols = slice(half * BANK, (half + 1) * BANK)
                    for n in range(NT):
                        nc.vector.scalar_tensor_tensor(out=x[:, n, cols], in0=accp[:, 2 * n + half, :],
                                                       scalar=combine[:, n, ds(e, 1)], in1=x[:, n, cols],
                                                       op0=ALU.mult, op1=ALU.add).then_inc(acc_added, 1)

            dve.wait_ge(acc_added, added(E))
            dve.wait_ge(ln_reloaded, 32 * 3)
            for n in range(NT):
                statistics(x[:, n, :], n, 2 + n, D, LN_EPS, ln_var)
            for n in range(NT):
                last = nc.vector.scalar_tensor_tensor(out=x[:, n, :], in0=x[:, n, :], scalar=mv[n][:, 0:1],
                                                      in1=ln_rows[:, 0, :], op0=ALU.subtract, op1=ALU.mult)
                if n == 0:
                    last.then_inc(out_scaled, 1)
            step(last)
            dve.wait_ge(ln_rstd, NT * 3 + 2)
            for n, half in ((0, 1), (1, 0), (1, 1)):
                cols = slice(half * BANK, (half + 1) * BANK)
                nc.vector.scalar_tensor_tensor(out=x[:, n, cols], in0=x[:, n, cols], scalar=rstd[:, 2 + n:3 + n],
                                               in1=ln_rows[:, 1, cols], op0=ALU.mult, op1=ALU.add).then_inc(out1_ready, 1)

        @block.tensor
        def _(pe):
            def split(p, e=0):
                pe.wait_ge(split_done, upto(p, e))
                return w_hi[:, p % PARTS, :], w_lo[:, p % PARTS, :]

            def split_columns(p):
                return [a.rearrange("p (k f) -> p k f", k=KD) for a in split(p)]

            def split_rows(p, e=0):
                return [a.rearrange("p (j d) -> p j d", j=2) for a in split(p, e)]

            def product(to, left, right, start, stop, **group):
                (lh, ll), (rh, rl) = left, right
                nc.tensor.matmul(to, lh, rh, start=start, stop=False, **group)
                nc.tensor.matmul(to, lh, rl, start=False, stop=False, **group)
                return nc.tensor.matmul(to, ll, rh, start=False, stop=stop, **group)

            def transpose_x(build, n):
                if build == 0:
                    pe.wait_ge(x_loaded[n], 16)
                for half in range(2):
                    if build:
                        pe.wait_ge(ln_norm, transposed(build - 1, n, half))
                    for k in range(4):
                        cols = slice((4 * half + k) * P, (4 * half + k + 1) * P)
                        last = nc.tensor.transpose(turn[:, 2 * n + half, k * P:(k + 1) * P], x[:, n, cols], ident[:])
                    last.then_inc(x_transposed, 1)

            def two_blocks(p, to, build=None):
                wh, wl = split_columns(p)
                for b in range(2):
                    at = slice(b * P, (b + 1) * P)
                    for k in range(KD):
                        if build is not None and b == 0 and k in (0, KD // 2):
                            pe.wait_ge(xT_ready, transposed(build, NT - 1, 2 * k // KD))
                        last = product(to[:, b, :], (wh[:, k, at], wl[:, k, at]), (xT_hi[:, k, :], xT_lo[:, k, :]),
                                       k == 0, k == KD - 1)
                last.then_inc(piece_used, 1)

            def keep_clock(count, bank):
                for _ in range(count):
                    nc.tensor.matmul(turn[:, bank, :], a_hi[:, 0:P], a_hi[:, 0:BANK], start=True, stop=True)

            def rows_product(n, half, wd, left, first, last_one):
                cols = slice(half * BANK, (half + 1) * BANK)
                for j in range(2):
                    last = product(accp[:, 2 * n + half, :], [a[:, j, n * P:(n + 1) * P] for a in left],
                                   [a[:, j, cols] for a in wd], first and j == 0, last_one and j == 1)
                return last

            def two_rows(p, left, first, between=None):
                wd = split_rows(p)
                for n in range(NT):
                    for half in range(2):
                        last = rows_product(n, half, wd, left, first, False)
                    if between and n == 0:
                        between()
                last.then_inc(piece_used, 1)

            def last_rows(pieces, build):
                for n in range(NT):
                    for i, (p, left, ready) in enumerate(pieces):
                        if n == 0:
                            pe.wait_ge(*ready)
                        wd = split_rows(p)
                        for half in range(2):
                            if n and i and half:
                                transpose_x(build, 0)
                            last = rows_product(n, half, wd, left, False, i == 1)
                            if i and not (n and half):
                                last.then_inc(sum_done, 1)
                        if n:
                            last.then_inc(piece_used, 1)

            pe.wait_ge(ident_ready, 1)
            for n in range(NT):
                transpose_x(0, n)

            for l in range(DEPTH):
                at = l * MIX1_AT
                for n in range(NT):
                    for half in range(2):
                        wv = split_columns(at + half)
                        for k in range(KD):
                            if half == 0 and k in (0, KD // 2):
                                pe.wait_ge(xT_ready, transposed(2 * l, n, 2 * k // KD))
                            last = product(accp[:, n, half * HALF:(half + 1) * HALF],
                                           [a[:, k, n * P:(n + 1) * P] for a in (xT_hi, xT_lo)],
                                           [a[:, k, :] for a in wv], k == 0, k == KD - 1)
                        if n:
                            last.then_inc(piece_used, 1)
                        elif l and half == 0:
                            transpose_x(2 * l, 1)
                for i in range(2):
                    two_blocks(at + 2 + i, turn_half[:, 4 + 2 * i:6 + 2 * i, :])
                if l == 0:
                    pe.wait_ge(chan_loaded, 16 * 6)
                    pe.wait_ge(v_gelu, NT)
                    nc.tensor.transpose(accp[:, 1, 0:N_CHAN], chan_rows[:],
                                        ident[0:N_CHAN, 0:N_CHAN]).then_inc(chan_transposed, 1)
                    pe.wait_ge(ws_masked, 1)
                    for i in range(DEPTH * HEADS):
                        last = nc.tensor.transpose(accp[:, 2 + i // 4, (i % 4) * P:(i % 4 + 1) * P], ws_raw[:, i, :],
                                                   ident[:])
                    last.then_inc(ws_transposed, 1)
                for i in range(2):
                    two_blocks(at + 4 + i, turn_half[:, 2 * i:2 * i + 2, :])
                pe.wait_ge(cg_ready, 2 * (l + 1))
                for i in range(2):
                    two_blocks(at + 6 + i, turn_half[:, 4 + 2 * i:6 + 2 * i, :])
                pe.wait_ge(q_ready, 2 * (l + 1))
                two_blocks(at + 8, turn_half[:, 0:2, :])
                if l == 0:
                    pe.wait_ge(consts_ready, 1)
                    pe.wait_ge(mean_conv_ready, 1)
                for b in range(2):
                    pe.wait_ge(conv_squared, 2 * l + b + 1)
                    nc.tensor.matmul(accp[:, b, :], mean_conv[:], conv_sq[:, 2 * b:2 * b + 2, :].rearrange(
                        "p c t -> p (c t)"), start=True, stop=True).then_inc(conv_mean, 1)
                pe.wait_ge(v_ready, NT * (l + 1))
                if l == 0:
                    pe.wait_ge(wsT_ready, 1)
                for h in range(HEADS):
                    for n in range(NT):
                        last = nc.tensor.matmul(acc_half[:, CB + h, n * P:(n + 1) * P], v[:, n, h * P:(h + 1) * P],
                                                wsT[:, l * HEADS + h, :], start=True, stop=True)
                last.then_inc(z_done, 1)
                two_blocks(at + 9, turn_half[:, 2:4, :])

                def gmlp_means():
                    for b in range(2):
                        pe.wait_ge(gmlp_squared, 2 * l + b + 1)
                        nc.tensor.matmul(turn[:, 2 + b, :], mean_gmlp[:], gmlp_sq[:, 2 * b:2 * b + 2, :].rearrange(
                            "p c t -> p (c t)"), start=True, stop=True).then_inc(gmlp_mean, 1)

                pe.wait_ge(zb_ready, l + 1)
                def y_blocks(i):
                    return y_hi[:, 2 * i:2 * i + 2, :], y_lo[:, 2 * i:2 * i + 2, :]

                for i in range(2):
                    pe.wait_ge(y_ready, 4 * l + i + 1)
                    two_rows(at + 10 + i, y_blocks(i), i == 0, None if i else gmlp_means)
                last_rows([(at + 10 + i, y_blocks(i), (y_ready, 4 * l + i + 1)) for i in (2, 3)], 2 * l + 1)
                if l == 0:
                    keep_clock(12, 3)
                    transpose_x(1, 1)
                    keep_clock(8, 0)
                if l == 1:
                    break

                def h_blocks(i):
                    return h_hi[:, i % 2], h_lo[:, i % 2]

                for j in range(GROUPS):
                    for i, p in enumerate((dense_gate(j), dense_up(j))):
                        two_blocks(p, turn_half[:, 4 * (j % 2) + 2 * i:4 * (j % 2) + 2 * i + 2, :],
                                   None if i or j else 1)
                    if 0 < j < GROUPS - 1:
                        i = j - 1
                        pe.wait_ge(h_ready, i + 1)
                        two_rows(dense_down(i), h_blocks(i), i == 0)
                last_rows([(dense_down(i), h_blocks(i), (h_ready, i + 1)) for i in (GROUPS - 2, GROUPS - 1)], 2)
                keep_clock(8, 3)

            pe.wait_ge(wr_loaded, 16)
            for n in range(NT):
                if n:
                    transpose_x(3, 1)
                pe.wait_ge(low_affine[n], 3)
                pe.wait_ge(high_affine[n], 3)
                for k in range(KD):
                    last = nc.tensor.matmul(accp[:, 0, n * E:(n + 1) * E], xT[:, k, n * P:(n + 1) * P], wr[:, k, :],
                                            start=(k == 0), stop=(k == KD - 1))
            last.then_inc(logits_done, 1)
            keep_clock(5, 0)
            pe.wait_ge(mask_ready, 1)
            nc.tensor.matmul(accp[:, 1, 0:E], before[:], mask[:, 0, :], start=True, stop=True)
            nc.tensor.matmul(accp[:, 1, E:2 * E], before[:], mask[:, 1, :], start=True, stop=False)
            nc.tensor.matmul(accp[:, 1, E:2 * E], ones[:], mask[:, 0, :], start=False, stop=True)
            nc.tensor.matmul(accp[:, 1, 2 * E:3 * E], ones[:], mask[:, 0, :], start=True, stop=False)
            nc.tensor.matmul(accp[:, 1, 2 * E:3 * E], ones[:], mask[:, 1, :], start=False, stop=True).then_inc(pos_done, 1)
            keep_clock(5, 0)

            pe.wait_ge(counts_ready, 1)
            pe.wait_ge(x_lo_ready, NT)

            def gather(e, part, to, first_slot):
                for k in range(KD):
                    for n in range(NT):
                        last = nc.tensor.matmul(to[:, k, :], part[:, n, k * P:(k + 1) * P],
                                                pick[:, n, first_slot:first_slot + P], start=(n == 0), stop=(n == NT - 1))
                return last

            def gather_first(e):
                pe.wait_ge(pick_ready, e + 1)
                gather(e, x_hi, first_slots(0), 0).then_inc(gathered, 1)
                gather(e, x_lo, first_slots(2), 0).then_inc(gathered, 1)

            def expert(e, tiles):
                def transpose_pick():
                    for n in range(NT):
                        for o in range(tiles):
                            to = accp[:, 2 + n, 0:P] if tiles == 1 else accp[:, 2, o * TOK + n * P:o * TOK + (n + 1) * P]
                            last = nc.tensor.transpose(to, pick[:, n, o * P:(o + 1) * P].bitcast(f32), ident[:])
                        if tiles == 1 or n == NT - 1:
                            last.then_inc(slots_written, 1)

                def transpose_h(s):
                    pe.wait_ge(e_h, e * STEPS + (s + 1))
                    for o in range(tiles):
                        to = accp[:, 2 + s % 2, :] if tiles == 1 else turn[:, 2 * o, :]
                        src = h_e[:, s % 2 if tiles == 1 else o, :]
                        for b in range(COL // P):
                            last = nc.tensor.transpose(to[:, b * P:(b + 1) * P], src[:, b * P:(b + 1) * P], ident[:])
                    last.then_inc(e_hT, 1)

                def down(s):
                    pe.wait_ge(e_hT_lo, e * STEPS + (s + 1))
                    for half in range(2):
                        p = MOE_AT + step_down(s) + half
                        if s == STEPS - 1 and half:
                            down_last(p)
                            continue
                        wd = split_rows(p, e)
                        for j in range(2):
                            for o in range(tiles):
                                for c in range(2):
                                    last = down_product(s, half, wd, j, o, c)
                        last.then_inc(piece_used, 1)
                        if tiles == 1 and s == STEPS - 2 and half == 0:
                            transpose_h(STEPS - 1)

                def down_product(s, half, wd, j, o, c):
                    b = 2 * half + j
                    at = (s % 2 if tiles == 1 else o) * BANK + b * P
                    return product(accp[:, 2 * o + c, :], [a[:, at:at + P] for a in (hT_hi, hT_lo)],
                                   [a[:, j, c * BANK:(c + 1) * BANK] for a in wd],
                                   s == 0 and b == 0, s == STEPS - 1 and b == 3)

                def down_last(p):
                    wd = split_rows(p, e)
                    for c in range(2):
                        for j in range(2):
                            for o in range(tiles):
                                last = down_product(STEPS - 1, 1, wd, j, o, c)
                        last.then_inc(piece_used if c else half_summed, 1)

                def half_step(s, which):
                    for half in range(2):
                        p = MOE_AT + step_at(s) + 2 * which + half
                        w = [a.rearrange("p (k f) -> p k f", k=KD // 2) for a in split(p, e)]
                        for o in range(tiles):
                            to = turn[:, 2 * (s % 2 if tiles == 1 else o) + which, :]
                            for kk in range(KD // 2):
                                k = half * (KD // 2) + kk
                                last = product(to, [a[:, k, o * P:(o + 1) * P] for a in (xg_hi, xg_lo)],
                                               [a[:, kk, :] for a in w], k == 0, k == KD - 1)
                        last.then_inc(piece_used, 1)

                pe.wait_ge(xg_hi_ready, e + 1)
                pe.wait_ge(xg_lo_ready, e + 1)
                if tiles == 2:
                    pe.wait_ge(acc_added, added(e))
                    gather(e, x_hi, acc_half_tile(0), P)
                    gather(e, x_lo, acc_half_tile(2), P).then_inc(slots_written, 1)
                    pe.wait_ge(slots_read, e * 2 + 1)
                    transpose_pick()
                for s in range(STEPS):
                    half_step(s, 0)
                    if s == 0 and tiles == 1:
                        pe.wait_ge(acc_added, added(e))
                        transpose_pick()
                    if s and tiles == 1:
                        transpose_h(s - 1)
                    half_step(s, 1)
                    if s == 0:
                        pe.wait_ge(slots_read, e * 2 + 2)
                    if s:
                        down(s - 1)
                    if tiles == 2:
                        transpose_h(s)
                        pe.wait_ge(e_hT_lo, e * STEPS + (s + 1))
                down(STEPS - 1)
                with pe.If(e < E - 1):
                    gather_first(e + 1)
                for half in range(2):
                    pe.wait_ge(ys_ready, e * 2 + half + 1)
                    for n in range(NT):
                        for o in range(tiles):
                            for i, part in enumerate(out_half(tiles, half)):
                                last = nc.tensor.matmul(accp[:, 2 * n + half, :], pickT[:, o, n * P:(n + 1) * P],
                                                        part[:, o, :], start=(o == 0 and i == 0),
                                                        stop=(o == tiles - 1 and i == 1))
                    last.then_inc(scattered, 1)

            gather_first(0)
            with pe.Fori(0, E) as e:
                many = pe.value_load(count_i[0:1, ds(e, 1)], min_val=0, max_val=TOK)
                with pe.If(many > P):
                    expert(e, 2)
                with pe.Else():
                    expert(e, 1)


_INS = ["x", "w_in", "conv_w", "v_g", "v_b", "w_s", "b_s", "out_g", "w_out", "ln1_g", "ln1_b", "ln2_g", "ln2_b",
        "w_gate", "w_up", "w_down", "w_router", "we_gate", "we_up", "we_down"]


def kernel(**inputs):
    import numpy as np
    import concourse.bacc as bacc
    from concourse.bass_utils import run_bass_kernel_spmd

    nc = bacc.Bacc("TRN2", target_bir_lowering=False, num_devices=1)
    arrays, args = {}, []
    for name in _INS:
        a = np.ascontiguousarray(inputs[name])
        arrays[f"in_{name}"] = a
        args.append(nc.dram_tensor(f"in_{name}", a.shape, mybir.dt.from_np(a.dtype), kind="ExternalInput").ap())
    shape = arrays["in_x"].shape
    out = nc.dram_tensor("out_x", shape, mybir.dt.float32, kind="ExternalOutput").ap()
    hybrid_trunk_kernel(nc, *args, out)
    r = run_bass_kernel_spmd(nc, [arrays], core_ids=[0])
    return r.results[0]["out_x"]
```
